# Optimizing a Trainium2 kernel written in Bass

```python
import math
import jax, jax.numpy as jnp
from jax import lax
import numpy as np

D_MODEL = 1024
BATCH = 1
SEQ = 2048
DEPTH = 1

CHUNK = 64
N_MIXERS = 3
EPS = 1e-6
GLA_HEADS = 4
GLA_DK = D_MODEL // (2 * GLA_HEADS)
GLA_DV = D_MODEL // GLA_HEADS
GLA_RANK = 16
GLA_TAU = 16.0
SSD_DINNER = 2 * D_MODEL
SSD_HEADDIM = 64
SSD_HEADS = SSD_DINNER // SSD_HEADDIM
SSD_GROUPS = 8
SSD_HPG = SSD_HEADS // SSD_GROUPS
SSD_DSTATE = 128
SSD_CONV = 4
S5_GROUP = 16
S5_GROUPS = D_MODEL // S5_GROUP
S5_STATE = 64
FFN_HIDDEN = ((-(-8 * D_MODEL // 3)) + 255) // 256 * 256

kernel_name = 'chunk_causal_hybrid_gla_ssd_s5'

def _layers_of(mixer):
    return len(range(mixer, DEPTH, N_MIXERS))

def rmsnorm(x, g):
    xf = x.astype(jnp.float32)
    y = xf * lax.rsqrt(jnp.mean(xf * xf, axis=-1, keepdims=True) + EPS)
    return (y * g.astype(jnp.float32)).astype(x.dtype)

def causal_depthwise_conv(x, w, b):
    k = w.shape[0]
    out = lax.conv_general_dilated(
        x, w[:, None, :].astype(x.dtype), window_strides=(1,), padding=[(k - 1, 0)],
        dimension_numbers=('NWC', 'WIO', 'NWC'), feature_group_count=x.shape[-1])
    return out + b.astype(x.dtype)

def gla_mixer(h, w_in, w_a2, b_a, norm_g, w_out):
    bsz, seq, _ = h.shape
    nc = seq // CHUNK
    f32 = jnp.float32
    qk = GLA_HEADS * GLA_DK
    vd = GLA_HEADS * GLA_DV
    proj = h @ w_in
    q, k, v, r, a_low = jnp.split(proj, [qk, 2 * qk, 2 * qk + vd, 2 * qk + 2 * vd], axis=-1)
    log_a = jax.nn.log_sigmoid((a_low @ w_a2 + b_a).astype(f32)) / GLA_TAU

    def chunks(t, d):
        return t.reshape(bsz, nc, CHUNK, GLA_HEADS, d).astype(f32)

    q = chunks(q, GLA_DK) * (GLA_DK ** -0.5)
    k = chunks(k, GLA_DK)
    v = chunks(v, GLA_DV)
    lc = jnp.cumsum(chunks(log_a, GLA_DK), axis=2)
    lend = lc[:, :, -1:]
    q_fwd = q * jnp.exp(lc)
    k_fwd = k * jnp.exp(-lc)
    q_bwd = q * jnp.exp(-lc)
    k_bwd = k * jnp.exp(lc)
    s_past = jnp.einsum('bclhd,bcshd->bchls', q_fwd, k_fwd)
    s_future = jnp.einsum('bclhd,bcshd->bchls', q_bwd, k_bwd)
    past_mask = jnp.tril(jnp.ones((CHUNK, CHUNK), dtype=bool))
    scores = jnp.where(past_mask, s_past, s_future)
    o = jnp.einsum('bchls,bcshv->bclhv', scores, v)
    g_chunk = jnp.exp(lend[:, :, 0])
    d_state = jnp.einsum('bcshd,bcshv->bchdv', k * jnp.exp(lend - lc), v)

    def step(s, inp):
        g, ds = inp
        return g[..., None] * s + ds, s

    s0 = jnp.zeros((bsz, GLA_HEADS, GLA_DK, GLA_DV), f32)
    _, s_prev = lax.scan(step, s0, (jnp.moveaxis(g_chunk, 1, 0), jnp.moveaxis(d_state, 1, 0)))
    s_prev = jnp.moveaxis(s_prev, 0, 1)
    o = o + jnp.einsum('bclhd,bchdv->bclhv', q_fwd, s_prev)
    o = rmsnorm(o.reshape(bsz, seq, GLA_HEADS, GLA_DV), norm_g.reshape(GLA_HEADS, GLA_DV))
    o = o.reshape(bsz, seq, vd) * jax.nn.silu(r.astype(f32))
    return (o @ w_out).astype(h.dtype)

def ssd_mixer(h, w_in, conv_w, conv_b, dt_bias, a_log, d_skip, norm_g, w_out):
    bsz, seq, _ = h.shape
    nc = seq // CHUNK
    f32 = jnp.float32
    gn = SSD_GROUPS * SSD_DSTATE
    proj = h @ w_in
    z, xbc, dt = jnp.split(proj, [SSD_DINNER, 2 * SSD_DINNER + 2 * gn], axis=-1)
    xbc = jax.nn.silu(causal_depthwise_conv(xbc, conv_w, conv_b))
    xs, bm, cm = jnp.split(xbc, [SSD_DINNER, SSD_DINNER + gn], axis=-1)
    dt = jax.nn.softplus(dt.astype(f32) + dt_bias.astype(f32))
    da = dt * (-jnp.exp(a_log.astype(f32)))
    xs = xs.reshape(bsz, nc, CHUNK, SSD_GROUPS, SSD_HPG, SSD_HEADDIM).astype(f32)
    bm = bm.reshape(bsz, nc, CHUNK, SSD_GROUPS, SSD_DSTATE).astype(f32)
    cm = cm.reshape(bsz, nc, CHUNK, SSD_GROUPS, SSD_DSTATE).astype(f32)
    dt = dt.reshape(bsz, nc, CHUNK, SSD_GROUPS, SSD_HPG)
    cum = jnp.cumsum(da.reshape(bsz, nc, CHUNK, SSD_GROUPS, SSD_HPG), axis=2)
    cb = jnp.einsum('bclgn,bcsgn->bcgls', cm, bm)
    cum_h = jnp.moveaxis(cum, 2, -1)
    decay = jnp.exp(-jnp.abs(cum_h[..., :, None] - cum_h[..., None, :]))
    dt_h = jnp.moveaxis(dt, 2, -1)
    mix = cb[:, :, :, None] * decay * dt_h[..., None, :]
    y = jnp.einsum('bcgjls,bcsgjp->bclgjp', mix, xs)
    cum_end = cum[:, :, -1]
    xw = xs * (dt * jnp.exp(cum_end[:, :, None] - cum))[..., None]
    states = jnp.einsum('bcsgn,bcsgjp->bcgjpn', bm, xw)

    def step(hs, inp):
        a, s = inp
        return a[..., None, None] * hs + s, hs

    h0 = jnp.zeros((bsz, SSD_GROUPS, SSD_HPG, SSD_HEADDIM, SSD_DSTATE), f32)
    _, h_prev = lax.scan(step, h0, (jnp.moveaxis(jnp.exp(cum_end), 1, 0), jnp.moveaxis(states, 1, 0)))
    h_prev = jnp.moveaxis(h_prev, 0, 1)
    y = y + jnp.einsum('bclgn,bcgjpn->bclgjp', cm, h_prev) * jnp.exp(cum)[..., None]
    y = y + d_skip.astype(f32).reshape(SSD_GROUPS, SSD_HPG)[:, :, None] * xs
    y = y.reshape(bsz, seq, SSD_DINNER) * jax.nn.silu(z.astype(f32))
    gsz = SSD_DINNER // SSD_GROUPS
    y = rmsnorm(y.reshape(bsz, seq, SSD_GROUPS, gsz), norm_g.reshape(SSD_GROUPS, gsz))
    return (y.reshape(bsz, seq, SSD_DINNER) @ w_out).astype(h.dtype)

def _complex_linear_combine(e1, e2):
    a1r, a1i, b1r, b1i = e1
    a2r, a2i, b2r, b2i = e2
    ar = a2r * a1r - a2i * a1i
    ai = a2r * a1i + a2i * a1r
    br = a2r * b1r - a2i * b1i + b2r
    bi = a2r * b1i + a2i * b1r + b2i
    return ar, ai, br, bi

def s5_mixer(h, log_dt, a_re, a_im, b_re, b_im, c_re, c_im, d_skip, w_glu):
    bsz, seq, _ = h.shape
    f32 = jnp.float32
    u = h.reshape(bsz, seq, S5_GROUPS, S5_GROUP).astype(f32)
    step = jnp.exp(log_dt.astype(f32))[:, None]
    a_re = a_re.astype(f32)
    a_im = a_im.astype(f32)
    mag = jnp.exp(step * a_re)
    abar_re = mag * jnp.cos(step * a_im)
    abar_im = mag * jnp.sin(step * a_im)
    den = a_re * a_re + a_im * a_im
    num_re = abar_re - 1.0
    num_im = abar_im
    f_re = (num_re * a_re + num_im * a_im) / den
    f_im = (num_im * a_re - num_re * a_im) / den
    b_re = b_re.astype(f32)
    b_im = b_im.astype(f32)
    bb_re = f_re[..., None] * b_re - f_im[..., None] * b_im
    bb_im = f_re[..., None] * b_im + f_im[..., None] * b_re
    bu_re = jnp.einsum('gpc,blgc->blgp', bb_re, u)
    bu_im = jnp.einsum('gpc,blgc->blgp', bb_im, u)
    a_seq_re = jnp.broadcast_to(abar_re, bu_re.shape)
    a_seq_im = jnp.broadcast_to(abar_im, bu_im.shape)
    _, _, x_re, x_im = lax.associative_scan(
        _complex_linear_combine, (a_seq_re, a_seq_im, bu_re, bu_im), axis=1)
    y = (jnp.einsum('gcp,blgp->blgc', c_re.astype(f32), x_re)
         - jnp.einsum('gcp,blgp->blgc', c_im.astype(f32), x_im))
    y = y + d_skip.astype(f32).reshape(S5_GROUPS, S5_GROUP) * u
    y = jax.nn.gelu(y.reshape(bsz, seq, D_MODEL))
    val, gate = jnp.split(y @ w_glu, 2, axis=-1)
    return (val * jax.nn.sigmoid(gate)).astype(h.dtype)

def swiglu_ffn(h, w_gu, w_down):
    g, u = jnp.split(h @ w_gu, 2, axis=-1)
    return (jax.nn.silu(g) * u) @ w_down

def setup_inputs(seed: int = 0) -> dict:
    key = jax.random.key(seed)
    ks = iter(jax.random.split(key, 48))
    f32 = jnp.float32

    def nrm(shape, scale):
        return jax.random.normal(next(ks), shape, f32) * scale

    n_gla, n_ssd, n_s5 = _layers_of(0), _layers_of(1), _layers_of(2)
    qk = GLA_HEADS * GLA_DK
    vd = GLA_HEADS * GLA_DV
    gla_in = 2 * qk + 2 * vd + GLA_RANK
    gn = SSD_GROUPS * SSD_DSTATE
    ssd_conv_dim = SSD_DINNER + 2 * gn
    ssd_in = SSD_DINNER + ssd_conv_dim + SSD_HEADS

    x = jax.random.normal(next(ks), (BATCH, SEQ, D_MODEL), f32)
    norm_mix_g = 1.0 + nrm((DEPTH, D_MODEL), 0.01)
    norm_ffn_g = 1.0 + nrm((DEPTH, D_MODEL), 0.01)
    gla_w_in = nrm((n_gla, D_MODEL, gla_in), D_MODEL ** -0.5)
    gla_w_a2 = nrm((n_gla, GLA_RANK, qk), GLA_RANK ** -0.5)
    gla_b_a = nrm((n_gla, qk), 0.1)
    gla_norm_g = 1.0 + nrm((n_gla, vd), 0.01)
    gla_w_out = nrm((n_gla, vd, D_MODEL), vd ** -0.5)
    ssd_w_in = nrm((n_ssd, D_MODEL, ssd_in), D_MODEL ** -0.5)
    ssd_conv_w = nrm((n_ssd, SSD_CONV, ssd_conv_dim), SSD_CONV ** -0.5)
    ssd_conv_b = nrm((n_ssd, ssd_conv_dim), 0.02)
    dt0 = jnp.exp(jax.random.uniform(next(ks), (n_ssd, SSD_HEADS), f32, math.log(1e-3), math.log(1e-1)))
    ssd_dt_bias = dt0 + jnp.log(-jnp.expm1(-dt0))
    ssd_a_log = jnp.log(jax.random.uniform(next(ks), (n_ssd, SSD_HEADS), f32, 1.0, 16.0))
    ssd_d = 1.0 + nrm((n_ssd, SSD_HEADS), 0.1)
    ssd_norm_g = 1.0 + nrm((n_ssd, SSD_DINNER), 0.01)
    ssd_w_out = nrm((n_ssd, SSD_DINNER, D_MODEL), SSD_DINNER ** -0.5)
    s5_log_dt = jax.random.uniform(next(ks), (n_s5, S5_GROUPS), f32, math.log(1e-3), math.log(1e-1))
    n_idx = jnp.arange(S5_STATE, dtype=f32)
    s5_a_re = -0.5 + nrm((n_s5, S5_GROUPS, S5_STATE), 0.01)
    s5_a_im = jnp.pi * n_idx + nrm((n_s5, S5_GROUPS, S5_STATE), 0.01)
    bscale = (2.0 * S5_GROUP) ** -0.5
    s5_b_re = nrm((n_s5, S5_GROUPS, S5_STATE, S5_GROUP), bscale)
    s5_b_im = nrm((n_s5, S5_GROUPS, S5_STATE, S5_GROUP), bscale)
    cscale = (2.0 * S5_STATE) ** -0.5
    s5_c_re = nrm((n_s5, S5_GROUPS, S5_GROUP, S5_STATE), cscale)
    s5_c_im = nrm((n_s5, S5_GROUPS, S5_GROUP, S5_STATE), cscale)
    s5_d = 1.0 + nrm((n_s5, D_MODEL), 0.1)
    s5_w_glu = nrm((n_s5, D_MODEL, 2 * D_MODEL), D_MODEL ** -0.5)
    ffn_w_gu = nrm((DEPTH, D_MODEL, 2 * FFN_HIDDEN), D_MODEL ** -0.5)
    ffn_w_down = nrm((DEPTH, FFN_HIDDEN, D_MODEL), FFN_HIDDEN ** -0.5)
    final_norm_g = 1.0 + nrm((D_MODEL,), 0.01)
    return {
        'x': x, 'norm_mix_g': norm_mix_g, 'norm_ffn_g': norm_ffn_g,
        'gla_w_in': gla_w_in, 'gla_w_a2': gla_w_a2, 'gla_b_a': gla_b_a,
        'gla_norm_g': gla_norm_g, 'gla_w_out': gla_w_out,
        'ssd_w_in': ssd_w_in, 'ssd_conv_w': ssd_conv_w, 'ssd_conv_b': ssd_conv_b,
        'ssd_dt_bias': ssd_dt_bias, 'ssd_a_log': ssd_a_log, 'ssd_d': ssd_d,
        'ssd_norm_g': ssd_norm_g, 'ssd_w_out': ssd_w_out,
        's5_log_dt': s5_log_dt, 's5_a_re': s5_a_re, 's5_a_im': s5_a_im,
        's5_b_re': s5_b_re, 's5_b_im': s5_b_im, 's5_c_re': s5_c_re, 's5_c_im': s5_c_im,
        's5_d': s5_d, 's5_w_glu': s5_w_glu,
        'ffn_w_gu': ffn_w_gu, 'ffn_w_down': ffn_w_down, 'final_norm_g': final_norm_g,
    }

def reference(x, norm_mix_g, norm_ffn_g,
              gla_w_in, gla_w_a2, gla_b_a, gla_norm_g, gla_w_out,
              ssd_w_in, ssd_conv_w, ssd_conv_b, ssd_dt_bias, ssd_a_log, ssd_d, ssd_norm_g, ssd_w_out,
              s5_log_dt, s5_a_re, s5_a_im, s5_b_re, s5_b_im, s5_c_re, s5_c_im, s5_d, s5_w_glu,
              ffn_w_gu, ffn_w_down, final_norm_g):
    h = x
    for i in range(DEPTH):
        mixer, j = i % N_MIXERS, i // N_MIXERS
        hn = rmsnorm(h, norm_mix_g[i])
        if mixer == 0:
            y = gla_mixer(hn, gla_w_in[j], gla_w_a2[j], gla_b_a[j], gla_norm_g[j], gla_w_out[j])
        elif mixer == 1:
            y = ssd_mixer(hn, ssd_w_in[j], ssd_conv_w[j], ssd_conv_b[j], ssd_dt_bias[j],
                          ssd_a_log[j], ssd_d[j], ssd_norm_g[j], ssd_w_out[j])
        else:
            y = s5_mixer(hn, s5_log_dt[j], s5_a_re[j], s5_a_im[j], s5_b_re[j], s5_b_im[j],
                         s5_c_re[j], s5_c_im[j], s5_d[j], s5_w_glu[j])
        h = h + y.astype(h.dtype)
        h = h + swiglu_ffn(rmsnorm(h, norm_ffn_g[i]), ffn_w_gu[i], ffn_w_down[i]).astype(h.dtype)
    return rmsnorm(h, final_norm_g)


_drawn_inputs = setup_inputs


def setup_inputs(seed=0):
    import zlib

    import numpy as np

    out = dict(_drawn_inputs(seed))
    spreads = {}
    factors = {'norm_mix_g': 4.506, 'norm_ffn_g': 8.0, 'gla_norm_g': 8.0, 'final_norm_g': 6.232}
    for name, (base, spread) in spreads.items():
        noise = np.random.default_rng([zlib.crc32(name.encode()), seed]).standard_normal(out[name].shape)
        drawn = base * np.exp(spread * noise) if base else spread * noise
        out[name] = __import__('jax').numpy.asarray(drawn.astype(out[name].dtype))
    for name, factor in factors.items():
        out[name] = (out[name] * factor).astype(out[name].dtype)
    return out
```

```python
from contextlib import ExitStack

import concourse.bass as bass
from concourse import mybir

P = 128
F32 = mybir.dt.float32
F32R = mybir.dt.float32r
I32 = mybir.dt.int32
BF16 = mybir.dt.bfloat16
ALU = mybir.AluOpType
ACT = mybir.ActivationFunctionType

CHUNK = 64
EPS = 1e-6
TAU = 16.0


class Signal:

    def __init__(self, sem, per, size=1, opened=False):
        self.sem, self.per, self.size, self.opened = sem, per, size, opened

    def after(self, iteration, n=0):
        return (iteration * self.per + (self.per if self.opened else 0) + n) * self.size

    def open(self, eng):
        assert self.opened
        eng.sem_inc(self.sem, self.per * self.size)


def gla_layer(nc, x, norm_mix_g, norm_ffn_g, w_in, w_a2, b_a, gla_norm_g, w_out, w_gu, w_down, final_norm_g, out):
    _, SEQ, D = x.shape
    RANK, QK = w_a2.shape[1], w_a2.shape[2]
    VD = w_out.shape[1]
    HID = w_down.shape[1]
    DK = P
    H = QK // DK
    DV = VD // H
    T = 512
    NB = SEQ // T
    NT = T // P
    KD = D // P
    KV = VD // P
    NCH = HID // P
    GROUPS = (12, NCH - 12)
    HALF = D // 2
    assert T == 4 * P and KD == 8 and KV == 8 and DV == 2 * P and all(g % 2 == 0 for g in GROUPS)

    UNIT = 512
    PAIRS_HEAD = 2 + KD // 2
    PAIRS = H * PAIRS_HEAD + KV + 2 * NCH + NCH
    ROUNDS = PAIRS // 2
    ROUND_OUT = H * PAIRS_HEAD // 2
    assert PAIRS % 2 == 0 and PAIRS_HEAD % 2 == 0
    group_round, at = [], ROUND_OUT + KV // 2
    for g in GROUPS:
        group_round.append((at, at + g))
        at += g + g // 2
    assert at == ROUNDS

    q_w = w_in[0, :, 0:QK].rearrange("(k p) n -> p k n", p=P)
    k_w = w_in[0, :, QK:2 * QK].rearrange("(k p) n -> p k n", p=P)
    v_w = w_in[0, :, 2 * QK:2 * QK + VD].rearrange("(k p) n -> p k n", p=P)
    r_w = w_in[0, :, 2 * QK + VD:2 * QK + 2 * VD].rearrange("(k p) n -> p k n", p=P)
    a_w = w_in[0, :, 2 * QK + 2 * VD:].rearrange("(k p) n -> p k n", p=P)
    o_w = w_out[0].rearrange("(k p) n -> p k n", p=P)
    gu_w = w_gu[0].rearrange("(k p) n -> p k n", p=P)
    d_w = w_down[0].rearrange("(k p) n -> p k n", p=P)
    x_tok = x[0]
    out_tok = out[0]

    with ExitStack() as ctx:
        def sb(name, shape, dt=F32):
            return ctx.enter_context(nc.sbuf_tensor(name, shape, dt))

        def signal(name, per=1, size=1, opened=False):
            return Signal(ctx.enter_context(nc.semaphore(name)), per, size, opened)

        ident = sb("ident", [P, P])
        future = sb("future", [P, NT, CHUNK], I32)
        carry_mask = sb("carry_mask", [P, T])
        g_mix = sb("g_mix", [P, D])
        g_ffn = sb("g_ffn", [P, D])
        g_fin = sb("g_fin", [P, D])
        g_gla = sb("g_gla", [P, VD])
        b_gate = sb("b_gate", [P, H])
        wa2 = sb("wa2", [RANK, QK])
        wa_raw = sb("wa_raw", [P, KD, RANK])
        wa_hi = sb("wa_hi", [P, KD, P], F32R)
        wa_lo = sb("wa_lo", [P, KD, P], F32R)
        h = sb("h", [P, NT, D])
        xs = sb("xs", [P, 2, D])
        junk = sb("junk", [P, D], BF16)
        sumsq = sb("sumsq", [P, NT])
        rstd = sb("rstd", [P, NT])
        variance = sb("variance", [P, NT])
        newton = sb("newton", [P, NT])
        xT_hi = sb("xT_hi", [P, KD, T], F32R)
        xT_lo = sb("xT_lo", [P, KD, T], F32R)
        act_hi = sb("act_hi", [P, max(GROUPS), T], F32R)
        act_lo = sb("act_lo", [P, max(GROUPS), T], F32R)
        raw = sb("raw", [P, 2, 2, UNIT])
        ring_hi = sb("ring_hi", [P, 4, UNIT], F32R)
        ring_lo = sb("ring_lo", [P, 4, UNIT], F32R)
        aT = sb("aT", [RANK, T])
        lc = sb("lc", [P, H, T])
        lend = sb("lend", [P, H * NT])
        e_even = sb("e_even", [P, H, NT])
        e_odd = sb("e_odd", [P, H, NT + 1])
        ef = sb("ef", [P, T])
        ei = sb("ei", [P, T])
        qf = sb("qf", [P, T])
        qb = sb("qb", [P, T])
        kf = sb("kf", [P, T])
        kb = sb("kb", [P, T])
        k_tok = sb("k_tok", [P, T])
        v_sb = sb("v_sb", [P, NT, DV])
        r_gate = sb("r_gate", [P, NT, DV])
        scores = sb("scores", [P, NT, P])
        state = sb("state", [P, H, DV])
        state_in = sb("state_in", [P, NT, DV])
        og = sb("og", [P, NT, DV])
        silu, prod = ef, ei
        softlog, gate_min = qf, qb

        ps = ctx.enter_context(nc.psum_tensor("ps", [P, 8, UNIT], F32))

        consts_loaded = signal("consts_loaded", 7, 16)
        masks = signal("masks")
        wa_ready = signal("wa_ready")
        pool_init = signal("pool_init")
        dve_init = signal("dve_init")
        raw_loaded = [signal(f"raw_loaded{i}", 1, 32) for i in range(2)]
        unit_hi = [signal(f"unit_hi{i}") for i in range(4)]
        unit_split = [signal(f"unit_split{i}", opened=True) for i in range(4)]
        unit_used = [signal(f"unit_used{i}", opened=True) for i in range(4)]
        x_loaded = [signal(f"x_loaded{i}", 1, 16) for i in range(NT)]
        squared = signal("squared", NT)
        variance_done = signal("variance_done", opened=True)
        log_done = signal("log_done")
        root_guess = signal("root_guess")
        newton_done = signal("newton_done", 2)
        rstd_ready = signal("rstd_ready")
        xs_ready = signal("xs_ready", NT, opened=True)
        xs_turned = signal("xs_turned", NT)
        xT_hi_done = signal("xT_hi_done", 2 * NT)
        xT_lo_done = signal("xT_lo_done", 2 * NT)
        out_stored = [signal(f"out_stored{i}", NT // 2, 16, opened=True) for i in range(2)]
        a_done = signal("a_done")
        aT_done = signal("aT_done")
        z_done = signal("z_done")
        z_abs = signal("z_abs")
        z_exp = signal("z_exp")
        z_log = signal("z_log")
        z_min = signal("z_min")
        z_sub = signal("z_sub", opened=True)
        z_scan = signal("z_scan")
        odd_kept = signal("odd_kept")
        lend_done = signal("lend_done")
        ends_done = signal("ends_done", 2)
        lc_ready = signal("lc_ready")
        decays = signal("decays", 2)
        q_scaled = signal("q_scaled", 2)
        k_scaled = signal("k_scaled", 2, opened=True)
        v_done = signal("v_done", 2)
        r_exp = signal("r_exp")
        r_plus = signal("r_plus")
        r_inv = signal("r_inv")
        r_silu = signal("r_silu")
        r_done = signal("r_done", opened=True)
        kt_done = signal("kt_done")
        k_tok_done = signal("k_tok_done")
        past_done = signal("past_done")
        future_done = signal("future_done")
        past_copied = signal("past_copied", 2)
        scores_ready = signal("scores_ready", 2)
        ds_done = signal("ds_done", NT)
        state_in_done = signal("state_in_done", NT)
        state_done = signal("state_done", NT, opened=True)
        o_done = signal("o_done", NT, opened=True)
        og_done = signal("og_done", NT)
        oT_done = signal("oT_done", 2)
        oT_hi = signal("oT_hi", 2)
        oT_lo = signal("oT_lo", 2, opened=True)
        wo_done = signal("wo_done", 2 * (NT - 1))
        wo_added = signal("wo_added", 2 * NT)
        silu_done = signal("silu_done", opened=True)
        prod_done = signal("prod_done", opened=True)
        hid_hi = signal("hid_hi")
        hid_lo = signal("hid_lo", opened=True)
        down_done = signal("down_done", 4 * (NT - 1))
        down_added = signal("down_added", 4 * NT)

        block = ctx.enter_context(nc.Block())

        @block.sync
        def _(sp):
            def load_pair(i, p, parts):
                sp.wait_ge(unit_split[2 * p].sem, unit_split[2 * p].after(i))
                sp.wait_ge(unit_split[2 * p + 1].sem, unit_split[2 * p + 1].after(i))
                for dst, src in parts:
                    sp.dma_start(dst, src).then_inc(raw_loaded[p].sem, 16)

            def columns(i, p, w, start):
                load_pair(i, p, [(raw[:, p, u, :].rearrange("p (k n) -> p k n", k=4),
                                  w[:, 4 * u:4 * u + 4, bass.ds(start, P)]) for u in range(2)])

            def rows(i, p, w, k, start):
                load_pair(i, p, [(raw[:, p, u, :], w[:, k + u, start:start + UNIT]) for u in range(2)])

            def qk(i, hd):
                columns(i, 0, q_w, hd * DK)
                columns(i, 1, k_w, hd * DK)

            def vr(i, hd):
                for n in range(2):
                    for p in range(2):
                        k = 4 * n + 2 * p
                        load_pair(i + n, p, [(raw[:, p, :, 0:DV], v_w[:, k:k + 2, bass.ds(hd * DV, DV)]),
                                             (raw[:, p, :, DV:], r_w[:, k:k + 2, bass.ds(hd * DV, DV)])])

            with sp.Fori(0, NB) as b:
                first = b * ROUNDS
                qk(first, 0)
                with sp.Fori(0, H - 1) as hd:
                    vr(first + hd * (PAIRS_HEAD // 2) + 1, hd)
                    qk(first + hd * (PAIRS_HEAD // 2) + 3, hd + 1)
                vr(first + ROUND_OUT - 2, H - 1)
                for n in range(KV):
                    half, k2 = divmod(n, KV // 2)
                    rows(first + ROUND_OUT + n // 2, n % 2, o_w, 2 * k2, half * HALF)
                c0 = 0
                for size, (up_at, down_at) in zip(GROUPS, group_round):
                    with sp.Fori(0, size) as c:
                        columns(first + c + up_at, 0, gu_w, c * P + c0 * P)
                        columns(first + c + up_at, 1, gu_w, c * P + (c0 * P + HID))
                    for n in range(size):
                        half, k2 = divmod(n, size // 2)
                        rows(first + down_at + n // 2, n % 2, d_w, c0 + 2 * k2, half * HALF)
                    c0 += size

        @block.gpsimd
        def _(pool):
            def step(ins):
                pool_steps[0] += 1
                ins.then_inc(pool_init.sem, 1)
                pool.wait_ge(pool_init.sem, pool_steps[0])

            for split in unit_split:
                split.open(pool)
            pool_steps = [0]
            step(pool.memset(ident[:, :], 0.0))
            step(pool.memset(future[:, :, :], 1))
            step(pool.memset(carry_mask[:, :], 1.0))
            step(pool.memset(wa_hi[:, :, :].bitcast(F32), 0.0))
            step(pool.memset(wa_lo[:, :, :].bitcast(F32), 0.0))
            step(pool.affine_select(out=ident[:, :], in_=ident[:, :], compare_op=ALU.not_equal, fill=1.0,
                                    base=0, pattern=[[-1, P]], channel_multiplier=1))
            for half in range(2):
                rows_ = future[half * CHUNK:(half + 1) * CHUNK, :, :]
                step(pool.affine_select(out=rows_, in_=rows_, compare_op=ALU.is_gt, fill=0.0, base=0,
                                        pattern=[[0, NT], [-1, CHUNK]], channel_multiplier=1))
            pool.memset(carry_mask[:, :].rearrange("p (c l) -> p c l", l=CHUNK)[:, :, 0:1], 0.0).then_inc(masks.sem, 1)
            pool.wait_ge(consts_loaded.sem, consts_loaded.after(1))
            step(pool.tensor_copy(wa_hi[:, :, 0:RANK], wa_raw[:, :, :]))
            pool.tensor_tensor(wa_lo[:, :, 0:RANK], wa_raw[:, :, :], wa_hi[:, :, 0:RANK].bitcast(F32),
                               ALU.subtract).then_inc(wa_ready.sem, 1)

            with pool.Fori(0, NB * ROUNDS) as i:
                for u in range(4):
                    p = u // 2
                    if u % 2 == 0:
                        pool.wait_ge(raw_loaded[p].sem, raw_loaded[p].after(i, 1))
                    pool.wait_ge(unit_used[u].sem, unit_used[u].after(i))
                    pool.nop(nofuse=True)
                    pool.tensor_scalar(ring_hi[:, u, :], raw[:, p, u % 2, :], 1.0, 0.0, ALU.mult,
                                       ALU.add).then_inc(unit_hi[u].sem, 1)
                    pool.wait_ge(unit_hi[u].sem, unit_hi[u].after(i, 1))
                    pool.tensor_tensor(ring_lo[:, u, :], raw[:, p, u % 2, :], ring_hi[:, u, :].bitcast(F32),
                                       ALU.subtract).then_inc(unit_split[u].sem, 1)

        @block.tensor
        def _(pe):
            def three(out, l_hi, l_lo, r_hi, r_lo, first, last):
                pe.matmul(out, l_hi, r_hi, start=first, stop=False)
                pe.matmul(out, l_hi, r_lo, start=False, stop=False)
                return pe.matmul(out, l_lo, r_hi, start=False, stop=last)

            def column_units(i, p, out):
                for k in range(KD):
                    u = 2 * p + k // 4
                    if k % 4 == 0:
                        pe.wait_ge(unit_split[u].sem, unit_split[u].after(i, 1))
                    cols = slice((k % 4) * P, (k % 4 + 1) * P)
                    ins = three(out, ring_hi[:, u, cols], ring_lo[:, u, cols], xT_hi[:, k, :], xT_lo[:, k, :],
                                k == 0, k == KD - 1)
                    if k % 4 == 3:
                        ins.then_inc(unit_used[u].sem, 1)

            def row_unit(i, u, l_hi, l_lo, k, bank0, first, last, done=None):
                pe.wait_ge(unit_split[u].sem, unit_split[u].after(i, 1))
                for t in range(NT):
                    tok = slice(t * P, (t + 1) * P)
                    ins = three(ps[:, bank0 + t, :], l_hi[:, k, tok], l_lo[:, k, tok], ring_hi[:, u, :],
                                ring_lo[:, u, :], first, last)
                    if last and done is not None and t < NT - 1:
                        ins.then_inc(done.sem, 1)
                ins.then_inc(unit_used[u].sem, 1)

            def turn(s, s3):
                for t in range(NT):
                    pe.wait_ge(xs_ready.sem, xs_ready.after(s3, t + 1))
                    if t >= 2:
                        pe.wait_ge(xT_lo_done.sem, xT_lo_done.after(s, 2 * (t - 1)))
                    for k in range(KD):
                        ins = pe.transpose(ps[:, 2 * (t % 2) + k // 4, (k % 4) * P:(k % 4 + 1) * P],
                                           xs[:, t % 2, k * P:(k + 1) * P], ident[:, :])
                    ins.then_inc(xs_turned.sem, 1)
                pe.wait_ge(xT_lo_done.sem, xT_lo_done.after(s, 2 * NT))
                pe.nop(nofuse=True)

            def qk(i, hd):
                pe.wait_ge(state_done.sem, state_done.after(hd))
                column_units(i, 0, ps[:, 0, :])
                column_units(i, 1, ps[:, 1, :])

            def vr_half(i, n):
                for u in range(4):
                    row_unit(i, u, xT_hi, xT_lo, 4 * n + u, 2, n + u == 0, n == 1 and u == 3)

            def attend(i, hd):
                pe.wait_ge(r_done.sem, r_done.after(hd))
                vr_half(i, 0)
                pe.wait_ge(k_scaled.sem, k_scaled.after(hd, 2))
                for t in range(NT):
                    tok = slice(t * P, (t + 1) * P)
                    ins = pe.transpose(ps[:, 0, tok], kf[:, tok], ident[:, :])
                ins.then_inc(kt_done.sem, 1)
                pe.wait_ge(oT_lo.sem, oT_lo.after(hd))
                for t in range(NT):
                    tok = slice(t * P, (t + 1) * P)
                    ins = pe.matmul(ps[:, 6, tok], kf[:, tok], qf[:, tok], start=True, stop=True)
                ins.then_inc(past_done.sem, 1)
                for t in range(NT):
                    tok = slice(t * P, (t + 1) * P)
                    ins = pe.matmul(ps[:, 7, tok], kb[:, tok], qb[:, tok], start=True, stop=True)
                ins.then_inc(future_done.sem, 1)
                vr_half(i + 1, 1)
                pe.wait_ge(k_tok_done.sem, k_tok_done.after(hd, 1))
                for t in range(NT):
                    pe.wait_ge(v_done.sem, v_done.after(hd, t // 2 + 1))
                    cols = slice((t % 2) * DV, (t % 2 + 1) * DV)
                    pe.matmul(ps[:, t // 2, cols], k_tok[:, t * P:(t + 1) * P], v_sb[:, t, :], start=True,
                              stop=True).then_inc(ds_done.sem, 1)
                pe.wait_ge(scores_ready.sem, scores_ready.after(hd, 2))
                for t in range(NT):
                    pe.wait_ge(state_in_done.sem, state_in_done.after(hd, t + 1))
                    o = ps[:, 6 + t // 2, (t % 2) * DV:(t % 2 + 1) * DV]
                    pe.matmul(o, scores[:, t, :], v_sb[:, t, :], start=True, stop=False)
                    pe.matmul(o, qf[:, t * P:(t + 1) * P], state_in[:, t, :], start=False,
                              stop=True).then_inc(o_done.sem, 1)

            def turn_o(hd):
                pe.wait_ge(og_done.sem, og_done.after(hd, NT))
                for j in range(2):
                    for t in range(NT):
                        ins = pe.transpose(ps[:, 6 + j, t * P:(t + 1) * P], og[:, t, j * P:(j + 1) * P], ident[:, :])
                    ins.then_inc(oT_done.sem, 1)

            for sig in (*unit_used, o_done):
                sig.open(pe)
            pe.wait_ge(masks.sem, masks.after(1))
            pe.wait_ge(wa_ready.sem, wa_ready.after(1))
            pe.wait_ge(consts_loaded.sem, consts_loaded.after(1))
            pe.wait_ge(dve_init.sem, dve_init.after(0, 1))
            with pe.Fori(0, NB) as b:
                first = b * ROUNDS
                turn(2 * b, 3 * b)

                for k in range(KD):
                    ins = three(ps[:, 4, :], wa_hi[:, k, :], wa_lo[:, k, :], xT_hi[:, k, :], xT_lo[:, k, :],
                                k == 0, k == KD - 1)
                ins.then_inc(a_done.sem, 1)
                pe.wait_ge(aT_done.sem, aT_done.after(b, 1))
                for hd in range(H):
                    pe.matmul(ps[:, hd, :], wa2[:, hd * DK:(hd + 1) * DK], aT[:, :], start=True,
                              stop=True).then_inc(z_done.sem, 1)
                pe.wait_ge(z_min.sem, z_min.after(b * H, H))

                qk(first, b * H)
                with pe.Fori(0, H - 1) as hh:
                    i = first + hh * (PAIRS_HEAD // 2)
                    attend(i + 1, b * H + hh)
                    qk(i + 3, b * H + hh + 1)
                    turn_o(b * H + hh)
                last = b * H + (H - 1)
                attend(first + ROUND_OUT - 2, last)

                pe.wait_ge(state_done.sem, state_done.after(last, NT))
                pe.wait_ge(r_done.sem, r_done.after(last, 1))
                pe.wait_ge(oT_lo.sem, oT_lo.after(last))
                for n in range(2 * KV):
                    half, k = divmod(n, KV)
                    if n == KV - 2:
                        turn_o(last)
                        pe.wait_ge(oT_lo.sem, oT_lo.after(last, 2))
                    row_unit(first + ROUND_OUT + n // 4, n % 4, act_hi, act_lo, k, 4 * half, k == 0, k == KV - 1,
                             wo_done)

                turn(2 * b + 1, 3 * b + 1)

                c0 = 0
                for g, (size, (up_at, down_at)) in enumerate(zip(GROUPS, group_round)):
                    if g > 0:
                        pe.wait_ge(down_added.sem, down_added.after(b, (2 * g - 1) * NT))
                        pe.nop(nofuse=True)
                    with pe.Fori(0, size) as c:
                        chunk = b * NCH + c + c0
                        pe.wait_ge(silu_done.sem, silu_done.after(chunk))
                        column_units(first + c + up_at, 0, ps[:, 0, :])
                        pe.wait_ge(prod_done.sem, prod_done.after(chunk))
                        column_units(first + c + up_at, 1, ps[:, 1, :])
                    pe.wait_ge(hid_lo.sem, hid_lo.after(b * NCH, c0 + size))
                    pe.nop(nofuse=True)
                    for n in range(2 * size):
                        half, k = divmod(n, size)
                        if k == 0 and half == 1:
                            if g == 0:
                                pe.wait_ge(wo_added.sem, wo_added.after(b, 2 * NT))
                            else:
                                pe.wait_ge(down_added.sem, down_added.after(b, 2 * g * NT))
                        row_unit(first + down_at + n // 4, n % 4, act_hi, act_lo, k, 4 * half, k == 0,
                                 k == size - 1, down_done)
                    c0 += size

        @block.scalar
        def _(act):
            def split_hi(dst, src):
                return act.activation(dst, src, ACT.Copy)

            def root(s7, n):
                act.wait_ge(variance_done.sem, variance_done.after(s7, 1))
                act.activation(rstd[:, :], variance[:, :], ACT.Ln).then_inc(log_done.sem, 1)
                act.wait_ge(log_done.sem, log_done.after(s7, 1))
                act.activation(rstd[:, :], rstd[:, :], ACT.Exp, scale=-0.5).then_inc(root_guess.sem, 1)

            def square_tiles(s7, arrived):
                act.wait_ge(variance_done.sem, variance_done.after(s7))
                for t in range(NT):
                    arrived(t)
                    act.activation(junk[:, :], h[:, t, :], ACT.Square,
                                   accum_out=sumsq[:, t:t + 1]).then_inc(squared.sem, 1)
                    act.wait_ge(squared.sem, squared.after(s7, t + 1))

            def turned_hi(s):
                for t in range(NT):
                    act.wait_ge(xs_turned.sem, xs_turned.after(s, t + 1))
                    for j in range(2):
                        split_hi(xT_hi[:, 4 * j:4 * j + 4, t * P:(t + 1) * P],
                                 ps[:, 2 * (t % 2) + j, :].rearrange("p (k n) -> p k n", n=P))\
                            .then_inc(xT_hi_done.sem, 1)

            for sig in (*out_stored, silu_done):
                sig.open(act)
            for dst, src in ((g_mix, norm_mix_g), (g_ffn, norm_ffn_g), (g_gla, gla_norm_g),
                             (g_fin, final_norm_g.rearrange("(a n) -> a n", a=1))):
                act.dma_start(dst[:, :], src.to_broadcast([P, src.shape[1]])).then_inc(consts_loaded.sem, 16)
            act.dma_start(wa_raw[:, :, :], a_w).then_inc(consts_loaded.sem, 16)
            act.dma_start(wa2[:, :], w_a2[0]).then_inc(consts_loaded.sem, 16)
            with nc.allow_non_contiguous_dma(reason="512 numbers, once"):
                act.dma_start(b_gate[:, :], b_a[0].rearrange("(h p) -> p h", p=P)).then_inc(consts_loaded.sem, 16)
            act.wait_ge(consts_loaded.sem, consts_loaded.after(1))
            act.wait_ge(dve_init.sem, dve_init.after(0, 1))
            with act.Fori(0, NB) as b:
                act.wait_ge(xs_ready.sem, xs_ready.after(3 * b))
                for t in range(NT):
                    act.dma_start(h[:, t, :], x_tok[bass.ds(b * T + t * P, P), :]).then_inc(x_loaded[t].sem, 16)
                square_tiles(7 * b, lambda t: act.wait_ge(x_loaded[t].sem, x_loaded[t].after(b, 1)))
                root(7 * b, D)
                turned_hi(2 * b)

                act.wait_ge(a_done.sem, a_done.after(b, 1))
                act.activation(aT[:, :], ps[0:RANK, 4, :], ACT.Copy).then_inc(aT_done.sem, 1)
                for hd in range(H):
                    act.wait_ge(z_done.sem, z_done.after(b * H, hd + 1))
                    act.wait_ge(z_sub.sem, z_sub.after(b * H, hd))
                    act.activation(softlog[:, :], ps[:, hd, :], ACT.Abs, bias=b_gate[:, hd:hd + 1])\
                        .then_inc(z_abs.sem, 1)
                    act.wait_ge(z_abs.sem, z_abs.after(b * H, hd + 1))
                    act.activation(softlog[:, :], softlog[:, :], ACT.Exp, scale=-1.0).then_inc(z_exp.sem, 1)
                    act.wait_ge(z_exp.sem, z_exp.after(b * H, hd + 1))
                    act.activation(softlog[:, :], softlog[:, :], ACT.Ln, bias=1.0).then_inc(z_log.sem, 1)
                ends = lc[:, :, :].rearrange("p h (t c l) -> p h t c l", c=2, l=CHUNK)[:, :, :, :, CHUNK - 1]
                act.wait_ge(z_scan.sem, z_scan.after(b * H, H))
                act.wait_ge(odd_kept.sem, odd_kept.after(b, 1))
                act.activation(e_even[:, :, :], ends[:, :, :, 0], ACT.Exp, scale=1 / TAU).then_inc(ends_done.sem, 1)
                act.activation(e_odd[:, :, 1:], ends[:, :, :, 1], ACT.Exp, scale=1 / TAU).then_inc(ends_done.sem, 1)
                act.wait_ge(lc_ready.sem, lc_ready.after(b, 1))

                with act.Fori(0, H) as hh:
                    hd = b * H + hh
                    i = b * ROUNDS + hh * (PAIRS_HEAD // 2)
                    act.wait_ge(k_scaled.sem, k_scaled.after(hd))
                    act.nop(nofuse=True)
                    row = lc[:, bass.ds(hh, 1), :].rearrange("p a l -> p (a l)")
                    act.activation(ef[:, :], row, ACT.Exp, scale=1 / TAU).then_inc(decays.sem, 1)
                    act.activation(ei[:, :], row, ACT.Exp, scale=-1 / TAU).then_inc(decays.sem, 1)
                    act.wait_ge(kt_done.sem, kt_done.after(hd, 1))
                    act.activation(k_tok[:, :], ps[:, 0, :], ACT.Copy).then_inc(k_tok_done.sem, 1)
                    act.wait_ge(past_done.sem, past_done.after(hd, 1))
                    past = ps[:, 6, :].rearrange("p (t n) -> p t n", n=P)
                    act.activation(scores[0:CHUNK, :, :], past[0:CHUNK, :, :], ACT.Copy).then_inc(past_copied.sem, 1)
                    act.activation(scores[CHUNK:, :, CHUNK:], past[CHUNK:, :, CHUNK:], ACT.Copy)\
                        .then_inc(past_copied.sem, 1)
                    act.wait_ge(unit_used[3].sem, unit_used[3].after(i + 2, 1))
                    for j in range(2):
                        act.activation(v_sb[:, 2 * j:2 * j + 2, :], ps[:, 2 + 2 * j:4 + 2 * j, 0:DV], ACT.Copy)\
                            .then_inc(v_done.sem, 1)
                    act.activation(r_gate[:, :, :], ps[:, 2:6, DV:], ACT.Exp, scale=-1.0).then_inc(r_exp.sem, 1)
                    s7 = b * 7 + hh + 1
                    act.wait_ge(variance_done.sem, variance_done.after(s7))
                    for t in range(NT):
                        act.wait_ge(o_done.sem, o_done.after(hd, 2 * (t // 2) + 2))
                        act.activation(junk[:, 0:DV], ps[:, 6 + t // 2, (t % 2) * DV:(t % 2 + 1) * DV], ACT.Square,
                                       accum_out=sumsq[:, t:t + 1]).then_inc(squared.sem, 1)
                        act.wait_ge(squared.sem, squared.after(s7, t + 1))
                    root(s7, DV)
                    for j in range(2):
                        act.wait_ge(oT_done.sem, oT_done.after(hd, j + 1))
                        act.nop(nofuse=True)
                        split_hi(act_hi[:, bass.ds(2 * hh + j, 1), :].rearrange("p a l -> p (a l)"), ps[:, 6 + j, :])\
                            .then_inc(oT_hi.sem, 1)

                square_tiles(7 * b + 5, lambda t: act.wait_ge(wo_added.sem, wo_added.after(b, NT + t + 1)))
                root(7 * b + 5, D)
                turned_hi(2 * b + 1)

                c0 = 0
                for size, (up_at, _) in zip(GROUPS, group_round):
                    with act.Fori(0, size) as c:
                        chunk = b * NCH + c + c0
                        i = b * ROUNDS + c + up_at
                        act.wait_ge(unit_used[1].sem, unit_used[1].after(i, 1))
                        act.wait_ge(prod_done.sem, prod_done.after(chunk))
                        act.activation(silu[:, :], ps[:, 0, :], ACT.Silu).then_inc(silu_done.sem, 1)
                        act.wait_ge(prod_done.sem, prod_done.after(chunk, 1))
                        act.nop(nofuse=True)
                        split_hi(act_hi[:, bass.ds(c, 1), :].rearrange("p a l -> p (a l)"), prod[:, :])\
                            .then_inc(hid_hi.sem, 1)
                    c0 += size

                square_tiles(7 * b + 6, lambda t: act.wait_ge(down_added.sem, down_added.after(b, 3 * NT + t + 1)))
                root(7 * b + 6, D)
                for t in range(NT):
                    act.wait_ge(xs_ready.sem, xs_ready.after(3 * b + 2, t + 1))
                    act.dma_start(out_tok[bass.ds(b * T + t * P, P), :], xs[:, t % 2, :])\
                        .then_inc(out_stored[t % 2].sem, 16)
            for stored in out_stored:
                act.wait_ge(stored.sem, stored.after(NB))

        @block.vector
        def _(dve):
            def split_lo(dst, src, hi):
                return dve.tensor_tensor(dst, src, hi.bitcast(F32), ALU.subtract)

            def root(s7, n):
                dve.wait_ge(squared.sem, squared.after(s7, NT))
                dve.tensor_scalar(variance[:, :], sumsq[:, :], 1 / n, EPS, ALU.mult, ALU.add)\
                    .then_inc(variance_done.sem, 1)
                dve.wait_ge(root_guess.sem, root_guess.after(s7, 1))
                dve.tensor_tensor(newton[:, :], rstd[:, :], rstd[:, :], ALU.mult).then_inc(newton_done.sem, 1)
                dve.wait_ge(newton_done.sem, newton_done.after(s7, 1))
                dve.scalar_tensor_tensor(out=newton[:, :], in0=newton[:, :], scalar=-0.5, in1=variance[:, :],
                                         op0=ALU.mult, op1=ALU.mult).then_inc(newton_done.sem, 1)
                dve.wait_ge(newton_done.sem, newton_done.after(s7, 2))
                dve.scalar_tensor_tensor(out=rstd[:, :], in0=newton[:, :], scalar=1.5, in1=rstd[:, :],
                                         op0=ALU.add, op1=ALU.mult).then_inc(rstd_ready.sem, 1)
                dve.wait_ge(rstd_ready.sem, rstd_ready.after(s7, 1))

            def turned_lo(s, t):
                for j in range(2):
                    dve.wait_ge(xT_hi_done.sem, xT_hi_done.after(s, 2 * t + j + 1))
                    blk = (slice(None), slice(4 * j, 4 * j + 4), slice(t * P, (t + 1) * P))
                    split_lo(xT_lo[blk], ps[:, 2 * (t % 2) + j, :].rearrange("p (k n) -> p k n", n=P), xT_hi[blk])\
                        .then_inc(xT_lo_done.sem, 1)

            def norm_and_turn(s7, s3, s, g, free_first):
                root(s7, D)
                for t in range(NT):
                    if t < 2:
                        free_first(t)
                    else:
                        turned_lo(s, t - 2)
                    dve.scalar_tensor_tensor(out=xs[:, t % 2, :], in0=h[:, t, :], scalar=rstd[:, t:t + 1],
                                             in1=g[:, :], op0=ALU.mult, op1=ALU.mult).then_inc(xs_ready.sem, 1)
                turned_lo(s, NT - 2)
                turned_lo(s, NT - 1)

            for sig in (state_done, r_done, oT_lo, prod_done, xs_ready, variance_done, k_scaled, hid_lo, z_sub):
                sig.open(dve)
            dve.memset(scores[:, :, :], 0.0)
            dve.memset(state[:, :, :], 0.0)
            dve.memset(e_odd[:, :, :], 1.0).then_inc(dve_init.sem, 1)
            dve.wait_ge(dve_init.sem, dve_init.after(0, 1))
            dve.wait_ge(consts_loaded.sem, consts_loaded.after(1))
            dve.wait_ge(masks.sem, masks.after(1))

            def add_rows(b, done, n, last_unit, last_round, half, added):
                for t in range(NT):
                    if t < NT - 1:
                        dve.wait_ge(done.sem, done.after(b, n + t + 1))
                    else:
                        dve.wait_ge(unit_used[last_unit].sem, unit_used[last_unit].after(last_round, 1))
                    hh = h[:, t, half * HALF:(half + 1) * HALF]
                    dve.tensor_tensor(hh, hh, ps[:, 4 * half + t, :], ALU.add).then_inc(added.sem, 1)

            with dve.Fori(0, NB) as b:
                first = b * ROUNDS
                norm_and_turn(7 * b, 3 * b, 2 * b, g_mix, lambda t: dve.wait_ge(out_stored[t % 2].sem, out_stored[t % 2].after(b)))
                for hd in range(H):
                    dve.wait_ge(z_abs.sem, z_abs.after(b * H, hd + 1))
                    dve.tensor_scalar(gate_min[:, :], ps[:, hd, :], b_gate[:, hd:hd + 1], 0.0, ALU.add, ALU.min)\
                        .then_inc(z_min.sem, 1)
                    dve.wait_ge(z_min.sem, z_min.after(b * H, hd + 1))
                    dve.wait_ge(z_log.sem, z_log.after(b * H, hd + 1))
                    dve.tensor_tensor(gate_min[:, :], gate_min[:, :], softlog[:, :], ALU.subtract)\
                        .then_inc(z_sub.sem, 1)
                    dve.wait_ge(z_sub.sem, z_sub.after(b * H, hd + 1))
                    dve.tensor_tensor_scan(lc[:, hd, :], carry_mask[:, :], gate_min[:, :], 0.0, ALU.mult,
                                           ALU.add).then_inc(z_scan.sem, 1)
                    dve.wait_ge(z_scan.sem, z_scan.after(b * H, hd + 1))
                dve.tensor_copy(e_odd[:, :, 0:1], e_odd[:, :, NT:]).then_inc(odd_kept.sem, 1)
                chunks = lc[:, :, :].rearrange("p h (t c l) -> p (h t) c l", c=2, l=CHUNK)
                dve.tensor_copy(lend[:, :], chunks[:, :, 0, CHUNK - 1]).then_inc(lend_done.sem, 1)
                dve.wait_ge(lend_done.sem, lend_done.after(b, 1))
                dve.wait_ge(ends_done.sem, ends_done.after(b, 2))
                dve.tensor_tensor(chunks[:, :, 0, :], chunks[:, :, 0, :],
                                  lend[:, :].unsqueeze(2).to_broadcast([P, H * NT, CHUNK]),
                                  ALU.subtract).then_inc(lc_ready.sem, 1)

                with dve.Fori(0, H) as hh:
                    hd = b * H + hh
                    i = first + hh * (PAIRS_HEAD // 2)
                    dve.wait_ge(decays.sem, decays.after(hd, 2))
                    dve.wait_ge(o_done.sem, o_done.after(hd))
                    dve.wait_ge(unit_used[1].sem, unit_used[1].after(i, 1))
                    dve.scalar_tensor_tensor(out=qf[:, :], in0=ps[:, 0, :], scalar=DK ** -0.5, in1=ef[:, :],
                                             op0=ALU.mult, op1=ALU.mult).then_inc(q_scaled.sem, 1)
                    dve.scalar_tensor_tensor(out=qb[:, :], in0=ps[:, 0, :], scalar=DK ** -0.5, in1=ei[:, :],
                                             op0=ALU.mult, op1=ALU.mult).then_inc(q_scaled.sem, 1)
                    dve.wait_ge(unit_used[3].sem, unit_used[3].after(i, 1))
                    dve.tensor_tensor(kf[:, :], ps[:, 1, :], ei[:, :], ALU.mult).then_inc(k_scaled.sem, 1)
                    dve.tensor_tensor(kb[:, :], ps[:, 1, :], ef[:, :], ALU.mult).then_inc(k_scaled.sem, 1)

                    dve.wait_ge(future_done.sem, future_done.after(hd, 1))
                    dve.wait_ge(past_copied.sem, past_copied.after(hd, 2))
                    dve.nop(nofuse=True)
                    back = ps[:, 7, :].rearrange("p (t n) -> p t n", n=P)
                    for c in range(2):
                        part = (slice(c * CHUNK, (c + 1) * CHUNK), slice(None), slice(c * CHUNK, (c + 1) * CHUNK))
                        dve.copy_predicated(scores[part], future[c * CHUNK:(c + 1) * CHUNK, :, :], back[part])\
                            .then_inc(scores_ready.sem, 1)

                    mine = state[:, bass.ds(hh, 1), :].rearrange("p a v -> p (a v)")
                    for t in range(NT):
                        if t > 0:
                            dve.wait_ge(state_done.sem, state_done.after(hd, t))
                        dve.tensor_scalar(state_in[:, t, :], mine, e_odd[:, bass.ds(hh, 1), t:t + 1].rearrange("p a t -> p (a t)"),
                                          e_even[:, bass.ds(hh, 1), t:t + 1].rearrange("p a t -> p (a t)"), ALU.mult,
                                          ALU.mult).then_inc(state_in_done.sem, 1)
                        dve.wait_ge(state_in_done.sem, state_in_done.after(hd, t + 1))
                        dve.wait_ge(ds_done.sem, ds_done.after(hd, 2 * (t // 2) + 2))
                        dve.tensor_tensor(mine, state_in[:, t, :], ps[:, t // 2, (t % 2) * DV:(t % 2 + 1) * DV],
                                          ALU.add).then_inc(state_done.sem, 1)

                    dve.wait_ge(r_exp.sem, r_exp.after(hd, 1))
                    dve.tensor_scalar(r_gate[:, :, :], r_gate[:, :, :], 1.0, None, ALU.add).then_inc(r_plus.sem, 1)
                    dve.wait_ge(r_plus.sem, r_plus.after(hd, 1))
                    dve.reciprocal(r_gate[:, :, :], r_gate[:, :, :]).then_inc(r_inv.sem, 1)
                    dve.wait_ge(r_inv.sem, r_inv.after(hd, 1))
                    dve.tensor_tensor(r_gate[:, :, :], r_gate[:, :, :], ps[:, 2:6, DV:], ALU.mult)\
                        .then_inc(r_silu.sem, 1)
                    dve.wait_ge(r_silu.sem, r_silu.after(hd, 1))
                    dve.tensor_tensor(r_gate[:, :, :], r_gate[:, :, :],
                                      g_gla[:, bass.ds(hh * DV, DV)].unsqueeze(1).to_broadcast([P, NT, DV]),
                                      ALU.mult).then_inc(r_done.sem, 1)
                    root(7 * b + hh + 1, DV)
                    dve.wait_ge(r_done.sem, r_done.after(hd, 1))
                    for t in range(NT):
                        dve.scalar_tensor_tensor(out=og[:, t, :], in0=ps[:, 6 + t // 2, (t % 2) * DV:(t % 2 + 1) * DV],
                                                 scalar=rstd[:, t:t + 1], in1=r_gate[:, t, :], op0=ALU.mult,
                                                 op1=ALU.mult).then_inc(og_done.sem, 1)
                    for j in range(2):
                        dve.wait_ge(oT_hi.sem, oT_hi.after(hd, j + 1))
                        split_lo(act_lo[:, bass.ds(2 * hh + j, 1), :].rearrange("p a l -> p (a l)"), ps[:, 6 + j, :],
                                 act_hi[:, bass.ds(2 * hh + j, 1), :].rearrange("p a l -> p (a l)"))\
                            .then_inc(oT_lo.sem, 1)

                for half in range(2):
                    add_rows(b, wo_done, half * (NT - 1), 3, first + ROUND_OUT + 2 * half + 1, half, wo_added)
                norm_and_turn(7 * b + 5, 3 * b + 1, 2 * b + 1, g_ffn, lambda t: None)

                c0 = 0
                for g, (size, (up_at, down_at)) in enumerate(zip(GROUPS, group_round)):
                    with dve.Fori(0, size) as c:
                        chunk = b * NCH + c + c0
                        dve.wait_ge(silu_done.sem, silu_done.after(chunk, 1))
                        dve.wait_ge(unit_used[3].sem, unit_used[3].after(first + c + up_at, 1))
                        dve.wait_ge(hid_lo.sem, hid_lo.after(chunk))
                        dve.tensor_tensor(prod[:, :], silu[:, :], ps[:, 1, :], ALU.mult).then_inc(prod_done.sem, 1)
                        dve.wait_ge(hid_hi.sem, hid_hi.after(chunk, 1))
                        split_lo(act_lo[:, bass.ds(c, 1), :].rearrange("p a l -> p (a l)"), prod[:, :],
                                 act_hi[:, bass.ds(c, 1), :].rearrange("p a l -> p (a l)")).then_inc(hid_lo.sem, 1)
                    for half in range(2):
                        n = (half + 1) * size - 1
                        add_rows(b, down_done, (2 * g + half) * (NT - 1), n % 4, first + down_at + n // 4, half,
                                 down_added)
                    c0 += size

                root(7 * b + 6, D)
                for t in range(NT):
                    if t >= 2:
                        dve.wait_ge(out_stored[t % 2].sem, out_stored[t % 2].after(b, 1))
                    dve.scalar_tensor_tensor(out=xs[:, t % 2, :], in0=h[:, t, :], scalar=rstd[:, t:t + 1],
                                             in1=g_fin[:, :], op0=ALU.mult, op1=ALU.mult).then_inc(xs_ready.sem, 1)


_INS = ["x", "norm_mix_g", "norm_ffn_g", "gla_w_in", "gla_w_a2", "gla_b_a", "gla_norm_g", "gla_w_out", "ffn_w_gu",
        "ffn_w_down", "final_norm_g"]


def kernel(**inputs):
    import numpy as np
    import concourse.bacc as bacc
    from concourse.bass_utils import run_bass_kernel_spmd

    nc = bacc.Bacc("TRN2", target_bir_lowering=False, num_devices=1)
    arrays, args = {}, []
    for name in _INS:
        a = np.ascontiguousarray(inputs[name])
        arrays[f"in_{name}"] = a
        args.append(nc.dram_tensor(f"in_{name}", a.shape, mybir.dt.from_np(a.dtype), kind="ExternalInput").ap())
    args.append(nc.dram_tensor("out_0", inputs["x"].shape, F32, kind="ExternalOutput").ap())
    gla_layer(nc, *args)
    return run_bass_kernel_spmd(nc, [arrays], core_ids=[0]).results[0]["out_0"]
```

```python
from contextlib import ExitStack

import concourse.bass as bass
from concourse import mybir

P = 128
F32 = mybir.dt.float32
F32R = mybir.dt.float32r
I32 = mybir.dt.int32
BF16 = mybir.dt.bfloat16
ALU = mybir.AluOpType
ACT = mybir.ActivationFunctionType

CHUNK = 64
EPS = 1e-6
TAU = 16.0


class Signal:

    def __init__(self, sem, per, size=1, opened=False):
        self.sem, self.per, self.size, self.opened = sem, per, size, opened

    def after(self, iteration, n=0):
        return (iteration * self.per + (self.per if self.opened else 0) + n) * self.size

    def open(self, eng):
        assert self.opened
        eng.sem_inc(self.sem, self.per * self.size)


def gla_layer(nc, x, norm_mix_g, norm_ffn_g, w_in, w_a2, b_a, gla_norm_g, w_out, w_gu, w_down, final_norm_g, out):
    _, SEQ, D = x.shape
    RANK, QK = w_a2.shape[1], w_a2.shape[2]
    VD = w_out.shape[1]
    HID = w_down.shape[1]
    DK = P
    H = QK // DK
    DV = VD // H
    T = 512
    NB = SEQ // T
    NT = T // P
    KD = D // P
    KV = VD // P
    NCH = HID // P
    GROUPS = (12, NCH - 12)
    HALF = D // 2
    assert T == 4 * P and KD == 8 and KV == 8 and DV == 2 * P and all(g % 2 == 0 for g in GROUPS)

    UNIT = 512
    PAIRS_HEAD = 2 + KD // 2
    PAIRS = H * PAIRS_HEAD + KV + 2 * NCH + NCH
    ROUNDS = PAIRS // 2
    ROUND_OUT = H * PAIRS_HEAD // 2
    assert PAIRS % 2 == 0 and PAIRS_HEAD % 2 == 0
    group_round, at = [], ROUND_OUT + KV // 2
    for g in GROUPS:
        group_round.append((at, at + g))
        at += g + g // 2
    assert at == ROUNDS
    TURN_AFTER = (1, 3, 6, 8)

    q_w = w_in[0, :, 0:QK].rearrange("(k p) n -> p k n", p=P)
    k_w = w_in[0, :, QK:2 * QK].rearrange("(k p) n -> p k n", p=P)
    v_w = w_in[0, :, 2 * QK:2 * QK + VD].rearrange("(k p) n -> p k n", p=P)
    r_w = w_in[0, :, 2 * QK + VD:2 * QK + 2 * VD].rearrange("(k p) n -> p k n", p=P)
    a_w = w_in[0, :, 2 * QK + 2 * VD:].rearrange("(k p) n -> p k n", p=P)
    o_w = w_out[0].rearrange("(k p) n -> p k n", p=P)
    gu_w = w_gu[0].rearrange("(k p) n -> p k n", p=P)
    d_w = w_down[0].rearrange("(k p) n -> p k n", p=P)
    x_tok = x[0]
    out_tok = out[0]

    with ExitStack() as ctx:
        def sb(name, shape, dt=F32):
            return ctx.enter_context(nc.sbuf_tensor(name, shape, dt))

        def signal(name, per=1, size=1, opened=False):
            return Signal(ctx.enter_context(nc.semaphore(name)), per, size, opened)

        ident = sb("ident", [P, P])
        future = sb("future", [P, NT, CHUNK], I32)
        carry_mask = sb("carry_mask", [P, T])
        g_mix = sb("g_mix", [P, D])
        g_ffn = sb("g_ffn", [P, D])
        g_fin = sb("g_fin", [P, D])
        g_gla = sb("g_gla", [P, VD])
        b_gate = sb("b_gate", [P, H])
        wa2 = sb("wa2", [RANK, QK])
        wa_raw = sb("wa_raw", [P, KD, RANK])
        wa_hi = sb("wa_hi", [P, KD, P], F32R)
        wa_lo = sb("wa_lo", [P, KD, P], F32R)
        h = sb("h", [P, NT, D])
        xs = sb("xs", [P, 2, D])
        junk = sb("junk", [P, D], BF16)
        sumsq = sb("sumsq", [P, NT])
        rstd = sb("rstd", [P, NT])
        variance = sb("variance", [P, NT])
        newton = sb("newton", [P, NT])
        xT_hi = sb("xT_hi", [P, KD, T], F32R)
        xT_lo = sb("xT_lo", [P, KD, T], F32R)
        act_hi = sb("act_hi", [P, max(GROUPS), T], F32R)
        act_lo = sb("act_lo", [P, max(GROUPS), T], F32R)
        raw = sb("raw", [P, 2, 2, UNIT])
        ring_hi = sb("ring_hi", [P, 4, UNIT], F32R)
        ring_lo = sb("ring_lo", [P, 4, UNIT], F32R)
        aT = sb("aT", [RANK, T])
        lc = sb("lc", [P, H, T])
        lend = sb("lend", [P, H * NT])
        e_even = sb("e_even", [P, H, NT])
        e_odd = sb("e_odd", [P, H, NT + 1])
        ef = sb("ef", [P, T])
        ei = sb("ei", [P, T])
        qk_scaled = sb("qk_scaled", [P, 4, T])
        qf, qb, kf, kb = (qk_scaled[:, n, :] for n in range(4))
        k_tok = sb("k_tok", [P, T])
        v_sb = sb("v_sb", [P, NT, DV])
        r_gate = sb("r_gate", [P, NT, DV])
        scores = sb("scores", [P, NT, P])
        state = sb("state", [P, H, DV])
        state_in = sb("state_in", [P, NT, DV])
        og = sb("og", [P, NT, DV])
        silu, prod = ef, ei
        softlog = qk_scaled

        ps = ctx.enter_context(nc.psum_tensor("ps", [P, 8, UNIT], F32))

        consts_loaded = signal("consts_loaded", 7, 16)
        masks = signal("masks")
        wa_ready = signal("wa_ready")
        pool_init = signal("pool_init")
        dve_init = signal("dve_init")
        raw_loaded = [signal(f"raw_loaded{i}", 1, 32) for i in range(2)]
        unit_hi = [signal(f"unit_hi{i}") for i in range(4)]
        unit_split = [signal(f"unit_split{i}", opened=True) for i in range(4)]
        unit_used = [signal(f"unit_used{i}", opened=True) for i in range(4)]
        x_in = [signal(f"x_in{i}", NT // 2, 16) for i in range(2)]
        h_loaded = [signal(f"h_loaded{i}", 1, 16) for i in range(NT)]
        squared = signal("squared", NT)
        variance_done = signal("variance_done")
        root_guess = signal("root_guess")
        newton_done = signal("newton_done", 3)
        rstd_ready = signal("rstd_ready")
        xs_ready = signal("xs_ready", NT)
        xs_turned = signal("xs_turned", NT)
        xT_hi_done = signal("xT_hi_done", 2 * NT)
        xT_lo_done = signal("xT_lo_done", 2 * NT)
        out_stored = [signal(f"out_stored{i}", NT // 2, 16, opened=True) for i in range(2)]
        a_done = signal("a_done")
        aT_done = signal("aT_done")
        z_done = signal("z_done", H)
        z_abs = signal("z_abs", H)
        z_min = signal("z_min", H)
        z_exp = signal("z_exp")
        z_log = signal("z_log")
        z_sub = signal("z_sub")
        z_scan = signal("z_scan", H)
        odd_kept = signal("odd_kept")
        lend_done = signal("lend_done")
        ends_done = signal("ends_done", 2)
        lc_ready = signal("lc_ready")
        decays = signal("decays", 2)
        q_scaled = signal("q_scaled", 2)
        k_scaled = signal("k_scaled", 2, opened=True)
        v_done = signal("v_done", 2)
        r_silu = signal("r_silu", opened=True)
        r_done = signal("r_done")
        kt_done = signal("kt_done")
        k_tok_done = signal("k_tok_done")
        past_done = signal("past_done")
        future_done = signal("future_done")
        past_copied = signal("past_copied", 2)
        scores_ready = signal("scores_ready", 2)
        ds_done = signal("ds_done", NT)
        state_in_done = signal("state_in_done", NT)
        state_done = signal("state_done", NT)
        o_done = signal("o_done", NT, opened=True)
        og_done = signal("og_done", NT)
        oT_done = signal("oT_done", 2)
        oT_hi = signal("oT_hi", 2)
        oT_lo = signal("oT_lo", 2, opened=True)
        wo_done = signal("wo_done", 2 * (NT - 1))
        wo_added = signal("wo_added", 2 * NT)
        silu_done = signal("silu_done", opened=True)
        prod_done = signal("prod_done", opened=True)
        hid_hi = signal("hid_hi")
        hid_lo = signal("hid_lo", opened=True)
        down_done = signal("down_done", 4 * (NT - 1))
        down_added = signal("down_added", 4 * NT, opened=True)

        def squares_pass(b, n):
            return b * (H + 3) + (n + 1)

        def root_number(b, n, t=0):
            return b * (H + 3 * NT) + (NT + n if isinstance(n, bass.RuntimeValue) or n < H
                                       else NT + H + (n - H) * NT + t)

        def xs_pass(b, n):
            return b * 3 + (n - H + 1)

        def turn_pass(b, n):
            return b * 2 + (n - H + 1)

        def next_rows(b):
            return ((b + 1) % NB) * T

        gate_up_banks = ((4, 5), (0, 1))

        def down_bank(g, half):
            return 4 * ((g + half) % 2)

        FFN, AHEAD, FINAL = H, H + 1, H + 2
        FIRST = dict(squares=0, roots=0, xs=0, turn=0, block=0)

        def passes(b, n):
            return dict(squares=squares_pass(b, n), roots=root_number(b, n), xs=xs_pass(b, n),
                        turn=turn_pass(b, n) if n != FINAL else None, block=b + 1)

        block = ctx.enter_context(nc.Block())

        @block.sync
        def _(sp):
            def load_pair(i, p, parts):
                sp.wait_ge(unit_split[2 * p].sem, unit_split[2 * p].after(i))
                sp.wait_ge(unit_split[2 * p + 1].sem, unit_split[2 * p + 1].after(i))
                for dst, src in parts:
                    sp.dma_start(dst, src).then_inc(raw_loaded[p].sem, 16)

            def columns(i, p, w, start):
                load_pair(i, p, [(raw[:, p, u, :].rearrange("p (k n) -> p k n", k=4),
                                  w[:, 4 * u:4 * u + 4, bass.ds(start, P)]) for u in range(2)])

            def rows(i, p, w, k, start):
                load_pair(i, p, [(raw[:, p, u, :], w[:, k + u, start:start + UNIT]) for u in range(2)])

            def qk(i, hd):
                columns(i, 0, q_w, hd * DK)
                columns(i, 1, k_w, hd * DK)

            def vr(i, hd):
                for n in range(2):
                    for p in range(2):
                        k = 4 * n + 2 * p
                        load_pair(i + n, p, [(raw[:, p, :, 0:DV], v_w[:, k:k + 2, bass.ds(hd * DV, DV)]),
                                             (raw[:, p, :, DV:], r_w[:, k:k + 2, bass.ds(hd * DV, DV)])])

            with sp.Fori(0, NB) as b:
                first = b * ROUNDS
                qk(first, 0)
                with sp.Fori(0, H - 1) as hd:
                    vr(first + hd * (PAIRS_HEAD // 2) + 1, hd)
                    qk(first + hd * (PAIRS_HEAD // 2) + 3, hd + 1)
                vr(first + ROUND_OUT - 2, H - 1)
                for n in range(KV):
                    half, k2 = divmod(n, KV // 2)
                    rows(first + ROUND_OUT + n // 2, n % 2, o_w, 2 * k2, half * HALF)
                c0 = 0
                for size, (up_at, down_at) in zip(GROUPS, group_round):
                    with sp.Fori(0, size) as c:
                        columns(first + c + up_at, 0, gu_w, c * P + c0 * P)
                        columns(first + c + up_at, 1, gu_w, c * P + (c0 * P + HID))
                    for n in range(size):
                        half, k2 = divmod(n, size // 2)
                        rows(first + down_at + n // 2, n % 2, d_w, c0 + 2 * k2, half * HALF)
                    c0 += size

        @block.gpsimd
        def _(pool):
            def step(ins):
                pool_steps[0] += 1
                ins.then_inc(pool_init.sem, 1)
                pool.wait_ge(pool_init.sem, pool_steps[0])

            for split in unit_split:
                split.open(pool)
            pool_steps = [0]
            step(pool.memset(ident[:, :], 0.0))
            step(pool.memset(future[:, :, :], 1))
            step(pool.memset(carry_mask[:, :], 1.0))
            step(pool.memset(wa_hi[:, :, :].bitcast(F32), 0.0))
            step(pool.memset(wa_lo[:, :, :].bitcast(F32), 0.0))
            step(pool.affine_select(out=ident[:, :], in_=ident[:, :], compare_op=ALU.not_equal, fill=1.0,
                                    base=0, pattern=[[-1, P]], channel_multiplier=1))
            for half in range(2):
                rows_ = future[half * CHUNK:(half + 1) * CHUNK, :, :]
                step(pool.affine_select(out=rows_, in_=rows_, compare_op=ALU.is_gt, fill=0.0, base=0,
                                        pattern=[[0, NT], [-1, CHUNK]], channel_multiplier=1))
            pool.memset(carry_mask[:, :].rearrange("p (c l) -> p c l", l=CHUNK)[:, :, 0:1], 0.0).then_inc(masks.sem, 1)
            pool.wait_ge(consts_loaded.sem, consts_loaded.after(1))
            step(pool.tensor_copy(wa_hi[:, :, 0:RANK], wa_raw[:, :, :]))
            pool.tensor_tensor(wa_lo[:, :, 0:RANK], wa_raw[:, :, :], wa_hi[:, :, 0:RANK].bitcast(F32),
                               ALU.subtract).then_inc(wa_ready.sem, 1)

            with pool.Fori(0, NB * ROUNDS) as i:
                for u in range(4):
                    p = u // 2
                    if u % 2 == 0:
                        pool.wait_ge(raw_loaded[p].sem, raw_loaded[p].after(i, 1))
                    pool.wait_ge(unit_used[u].sem, unit_used[u].after(i))
                    pool.nop(nofuse=True)
                    pool.tensor_scalar(ring_hi[:, u, :], raw[:, p, u % 2, :], 1.0, 0.0, ALU.mult,
                                       ALU.add).then_inc(unit_hi[u].sem, 1)
                    pool.wait_ge(unit_hi[u].sem, unit_hi[u].after(i, 1))
                    pool.tensor_tensor(ring_lo[:, u, :], raw[:, p, u % 2, :], ring_hi[:, u, :].bitcast(F32),
                                       ALU.subtract).then_inc(unit_split[u].sem, 1)

        @block.tensor
        def _(pe):
            def three(out, l_hi, l_lo, r_hi, r_lo, first, last):
                pe.matmul(out, l_hi, r_hi, start=first, stop=False)
                pe.matmul(out, l_hi, r_lo, start=False, stop=False)
                return pe.matmul(out, l_lo, r_hi, start=False, stop=last)

            def column_units(i, p, out):
                for k in range(KD):
                    u = 2 * p + k // 4
                    if k % 4 == 0:
                        pe.wait_ge(unit_split[u].sem, unit_split[u].after(i, 1))
                    cols = slice((k % 4) * P, (k % 4 + 1) * P)
                    ins = three(out, ring_hi[:, u, cols], ring_lo[:, u, cols], xT_hi[:, k, :], xT_lo[:, k, :],
                                k == 0, k == KD - 1)
                    if k % 4 == 3:
                        ins.then_inc(unit_used[u].sem, 1)

            def half_column_units(i, p, bank, tokens):
                tok = slice(tokens * T // 2, (tokens + 1) * T // 2)
                for k in range(KD):
                    u = 2 * p + k // 4
                    if k % 4 == 0 and tokens == 0:
                        pe.wait_ge(unit_split[u].sem, unit_split[u].after(i, 1))
                    cols = slice((k % 4) * P, (k % 4 + 1) * P)
                    ins = three(ps[:, bank, tok], ring_hi[:, u, cols], ring_lo[:, u, cols], xT_hi[:, k, tok],
                                xT_lo[:, k, tok], k == 0, k == KD - 1)
                    if k % 4 == 3 and tokens == 1:
                        ins.then_inc(unit_used[u].sem, 1)

            def row_unit(i, u, l_hi, l_lo, k, bank0, first, last, done=None):
                pe.wait_ge(unit_split[u].sem, unit_split[u].after(i, 1))
                for t in range(NT):
                    tok = slice(t * P, (t + 1) * P)
                    ins = three(ps[:, bank0 + t, :], l_hi[:, k, tok], l_lo[:, k, tok], ring_hi[:, u, :],
                                ring_lo[:, u, :], first, last)
                    if last and done is not None and t < NT - 1:
                        ins.then_inc(done.sem, 1)
                ins.then_inc(unit_used[u].sem, 1)

            def turn_tile(at, t, bank0):
                pe.wait_ge(xs_ready.sem, xs_ready.after(at["xs"], t + 1))
                if t >= 2:
                    pe.wait_ge(xT_lo_done.sem, xT_lo_done.after(at["turn"], 2 * (t - 1)))
                for k in range(KD):
                    ins = pe.transpose(ps[:, bank0 + 2 * (t % 2) + k // 4, (k % 4) * P:(k % 4 + 1) * P],
                                       xs[:, t % 2, k * P:(k + 1) * P], ident[:, :])
                ins.then_inc(xs_turned.sem, 1)

            def low_rank(at):
                pe.wait_ge(xT_lo_done.sem, xT_lo_done.after(at["turn"], 2 * NT))
                for k in range(KD):
                    ins = three(ps[:, 6, :], wa_hi[:, k, :], wa_lo[:, k, :], xT_hi[:, k, :], xT_lo[:, k, :],
                                k == 0, k == KD - 1)
                ins.then_inc(a_done.sem, 1)

            def vr_units(i, n, units):
                for u in units:
                    row_unit(i, u, xT_hi, xT_lo, 4 * n + u, 2, n + u == 0, n == 1 and u == 3)

            def make_scores(hd):
                pe.wait_ge(k_scaled.sem, k_scaled.after(hd, 2))
                for t in range(NT):
                    tok = slice(t * P, (t + 1) * P)
                    ins = pe.transpose(ps[:, 0, tok], kf[:, tok], ident[:, :])
                ins.then_inc(kt_done.sem, 1)
                pe.wait_ge(oT_lo.sem, oT_lo.after(hd))
                for t in range(NT):
                    tok = slice(t * P, (t + 1) * P)
                    ins = pe.matmul(ps[:, 6, tok], kf[:, tok], qf[:, tok], start=True, stop=True)
                ins.then_inc(past_done.sem, 1)
                for t in range(NT):
                    tok = slice(t * P, (t + 1) * P)
                    ins = pe.matmul(ps[:, 7, tok], kb[:, tok], qb[:, tok], start=True, stop=True)
                ins.then_inc(future_done.sem, 1)

            def use_scores(hd):
                for two in range(2):
                    pe.wait_ge(v_done.sem, v_done.after(hd, two + 1))
                    if two == 0:
                        pe.wait_ge(k_tok_done.sem, k_tok_done.after(hd, 1))
                    else:
                        pe.wait_ge(state_done.sem, state_done.after(hd, 2))
                    for t in (2 * two, 2 * two + 1):
                        pe.matmul(ps[:, 1, (t % 2) * DV:(t % 2 + 1) * DV], k_tok[:, t * P:(t + 1) * P],
                                  v_sb[:, t, :], start=True, stop=True).then_inc(ds_done.sem, 1)
                    if two == 0:
                        pe.wait_ge(scores_ready.sem, scores_ready.after(hd, 2))
                    for t in (2 * two, 2 * two + 1):
                        o = ps[:, 6 + two, (t % 2) * DV:(t % 2 + 1) * DV]
                        pe.matmul(o, scores[:, t, :], v_sb[:, t, :], start=True, stop=False)
                        pe.wait_ge(state_in_done.sem, state_in_done.after(hd, t + 1))
                        pe.matmul(o, qf[:, t * P:(t + 1) * P], state_in[:, t, :], start=False,
                                  stop=True).then_inc(o_done.sem, 1)

            def turn_o(hd):
                pe.wait_ge(og_done.sem, og_done.after(hd, NT))
                for j in range(2):
                    for t in range(NT):
                        ins = pe.transpose(ps[:, 6 + j, t * P:(t + 1) * P], og[:, t, j * P:(j + 1) * P], ident[:, :])
                    ins.then_inc(oT_done.sem, 1)

            for sig in (*unit_used, o_done):
                sig.open(pe)
            pe.wait_ge(masks.sem, masks.after(0, 1))
            pe.wait_ge(wa_ready.sem, wa_ready.after(0, 1))
            pe.wait_ge(consts_loaded.sem, consts_loaded.after(0, 7))
            pe.wait_ge(dve_init.sem, dve_init.after(0, 1))
            for t in range(NT):
                turn_tile(FIRST, t, 4)
            low_rank(FIRST)

            with pe.Fori(0, NB) as b:
                first = b * ROUNDS
                pe.wait_ge(down_added.sem, down_added.after(b))
                column_units(first, 0, ps[:, 0, :])
                pe.wait_ge(aT_done.sem, aT_done.after(b, 1))
                for hd in range(H):
                    pe.matmul(ps[:, 4 + hd, :], wa2[:, hd * DK:(hd + 1) * DK], aT[:, :], start=True,
                              stop=True).then_inc(z_done.sem, 1)
                column_units(first, 1, ps[:, 1, :])
                pe.wait_ge(z_min.sem, z_min.after(b, H))
                pe.wait_ge(r_silu.sem, r_silu.after(b * H))
                vr_units(first + 1, 0, range(4))

                with pe.Fori(0, H - 1) as hh:
                    hd = b * H + hh
                    i = first + hh * (PAIRS_HEAD // 2)
                    make_scores(hd)
                    vr_units(i + 2, 1, range(4))
                    pe.wait_ge(k_tok_done.sem, k_tok_done.after(hd, 1))
                    column_units(i + 3, 0, ps[:, 0, :])
                    use_scores(hd)
                    pe.wait_ge(state_done.sem, state_done.after(hd, NT))
                    column_units(i + 3, 1, ps[:, 1, :])
                    pe.wait_ge(r_silu.sem, r_silu.after(hd, 1))
                    vr_units(i + 4, 0, (0, 1))
                    turn_o(hd)
                    vr_units(i + 4, 0, (2, 3))
                last = b * H + (H - 1)
                make_scores(last)
                vr_units(first + ROUND_OUT - 1, 1, range(4))
                use_scores(last)

                pe.wait_ge(state_done.sem, state_done.after(last, NT))
                pe.wait_ge(r_silu.sem, r_silu.after(last, 1))
                pe.wait_ge(oT_lo.sem, oT_lo.after(last))
                for n in range(KV + 4):
                    half, k = divmod(n, KV)
                    if n == KV - 2:
                        turn_o(last)
                        pe.wait_ge(oT_lo.sem, oT_lo.after(last, 2))
                    row_unit(first + ROUND_OUT + n // 4, n % 4, act_hi, act_lo, k, 4 * half, k == 0, k == KV - 1,
                             wo_done)
                i = first + ROUND_OUT + 3
                for t in range(NT):
                    tok = slice(t * P, (t + 1) * P)
                    for u in range(4):
                        if t == 0:
                            pe.wait_ge(unit_split[u].sem, unit_split[u].after(i, 1))
                        ins = three(ps[:, 4 + t, :], act_hi[:, 4 + u, tok], act_lo[:, 4 + u, tok], ring_hi[:, u, :],
                                    ring_lo[:, u, :], False, u == 3)
                        if t == NT - 1:
                            ins.then_inc(unit_used[u].sem, 1)
                    if t < NT - 1:
                        ins.then_inc(wo_done.sem, 1)

                at = passes(b, FFN)
                i = first + group_round[0][0]
                turn_tile(at, 0, 0)
                turn_tile(at, 1, 0)
                pe.wait_ge(xT_lo_done.sem, xT_lo_done.after(at["turn"], 4))
                half_column_units(i, 0, 4, 0)
                turn_tile(at, 2, 0)
                half_column_units(i, 1, 5, 0)
                turn_tile(at, 3, 0)
                pe.wait_ge(xT_lo_done.sem, xT_lo_done.after(at["turn"], 8))
                half_column_units(i, 0, 4, 1)
                half_column_units(i, 1, 5, 1)

                ahead = passes(b, AHEAD)
                c0 = 0
                for g, (size, (up_at, down_at)) in enumerate(zip(GROUPS, group_round)):
                    gate, up = gate_up_banks[g]
                    if g > 0:
                        pe.wait_ge(down_added.sem, down_added.after(b, (2 * g - 1) * NT))
                        pe.nop(nofuse=True)
                    with pe.Fori(1 if g == 0 else 0, size) as c:
                        chunk = b * NCH + c + c0
                        pe.wait_ge(silu_done.sem, silu_done.after(chunk))
                        column_units(first + c + up_at, 0, ps[:, gate, :])
                        pe.wait_ge(prod_done.sem, prod_done.after(chunk))
                        column_units(first + c + up_at, 1, ps[:, up, :])
                    if g > 0:
                        pe.wait_ge(down_added.sem, down_added.after(b, 2 * g * NT))
                    pe.wait_ge(hid_lo.sem, hid_lo.after(b * NCH, c0 + size - 1))
                    pe.nop(nofuse=True)
                    for n in range(2 * size):
                        half, k = divmod(n, size)
                        if n == size - 1:
                            pe.wait_ge(hid_lo.sem, hid_lo.after(b * NCH, c0 + size))
                        row_unit(first + down_at + n // 4, n % 4, act_hi, act_lo, k, down_bank(g, half), k == 0,
                                 k == size - 1, down_done)
                        if g == len(GROUPS) - 1 and half == 1 and k in TURN_AFTER:
                            if k == TURN_AFTER[0]:
                                pe.wait_ge(down_added.sem, down_added.after(b, (2 * g + 1) * NT))
                            turn_tile(ahead, TURN_AFTER.index(k), 4)
                    c0 += size
                low_rank(ahead)

        @block.scalar
        def _(act):
            def split_hi(dst, src):
                return act.activation(dst, src, ACT.Copy)

            def root(n, cols=slice(0, NT)):
                act.wait_ge(variance_done.sem, variance_done.after(n, 1))
                act.activation(rstd[:, cols], variance[:, cols], ACT.Sqrt).then_inc(root_guess.sem, 1)

            def square(at, t, tile):
                if t > 0:
                    act.wait_ge(squared.sem, squared.after(at["squares"], t))
                act.activation(junk[:, :], tile, ACT.Square, accum_out=sumsq[:, t:t + 1]).then_inc(squared.sem, 1)

            def tile_root(at, t):
                root(at["roots"] + t, slice(t, t + 1))

            def turned_hi(at, t, bank0):
                act.wait_ge(xs_turned.sem, xs_turned.after(at["turn"], t + 1))
                for j in range(2):
                    split_hi(xT_hi[:, 4 * j:4 * j + 4, t * P:(t + 1) * P],
                             ps[:, bank0 + 2 * (t % 2) + j, :].rearrange("p (k n) -> p k n", n=P))\
                        .then_inc(xT_hi_done.sem, 1)

            def load_x(rows, t):
                act.dma_start(xs[:, t % 2, :], x_tok[bass.ds(rows + t * P, P), :]).then_inc(x_in[t % 2].sem, 16)

            def load_h(rows):
                for t in range(NT):
                    act.dma_start(h[:, t, :], x_tok[bass.ds(rows + t * P, P), :]).then_inc(h_loaded[t].sem, 16)

            def square_x(at, t):
                act.wait_ge(x_in[t % 2].sem, x_in[t % 2].after(at["block"], t // 2 + 1))
                square(at, t, xs[:, t % 2, :])

            def look_ahead(at, rows):
                for t in range(2):
                    square_x(at, t)
                    tile_root(at, t)
                for t in range(NT):
                    if t >= 2:
                        square_x(at, t)
                        tile_root(at, t)
                    turned_hi(at, t, 4)
                    if t < 2:
                        load_x(rows, t + 2)

            def copy_low_rank(block):
                act.wait_ge(a_done.sem, a_done.after(block, 1))
                act.activation(aT[:, :], ps[0:RANK, 6, :], ACT.Copy).then_inc(aT_done.sem, 1)

            def make_decays(hh, hd):
                act.wait_ge(k_scaled.sem, k_scaled.after(hd))
                act.nop(nofuse=True)
                row = lc[:, bass.ds(hh, 1), :].rearrange("p a l -> p (a l)")
                act.activation(ef[:, :], row, ACT.Exp, scale=1 / TAU).then_inc(decays.sem, 1)
                act.activation(ei[:, :], row, ACT.Exp, scale=-1 / TAU).then_inc(decays.sem, 1)

            def head(b, hh, hd, i, last):
                act.wait_ge(kt_done.sem, kt_done.after(hd, 1))
                act.activation(k_tok[:, :], ps[:, 0, :], ACT.Copy).then_inc(k_tok_done.sem, 1)
                act.wait_ge(past_done.sem, past_done.after(hd, 1))
                past = ps[:, 6, :].rearrange("p (t n) -> p t n", n=P)
                act.activation(scores[0:CHUNK, :, :], past[0:CHUNK, :, :], ACT.Copy).then_inc(past_copied.sem, 1)
                act.activation(scores[CHUNK:, :, CHUNK:], past[CHUNK:, :, CHUNK:], ACT.Copy)\
                    .then_inc(past_copied.sem, 1)
                act.wait_ge(unit_used[3].sem, unit_used[3].after(i + 2, 1))
                for j in range(2):
                    act.activation(v_sb[:, 2 * j:2 * j + 2, :], ps[:, 2 + 2 * j:4 + 2 * j, 0:DV], ACT.Copy)\
                        .then_inc(v_done.sem, 1)
                act.activation(r_gate[:, :, :], ps[:, 2:6, DV:], ACT.Silu).then_inc(r_silu.sem, 1)
                n = squares_pass(b, hh)
                for t in range(NT):
                    act.wait_ge(o_done.sem, o_done.after(hd, 2 * (t // 2) + 2))
                    if t > 0:
                        act.wait_ge(squared.sem, squared.after(n, t))
                    act.activation(junk[:, 0:DV], ps[:, 6 + t // 2, (t % 2) * DV:(t % 2 + 1) * DV], ACT.Square,
                                   accum_out=sumsq[:, t:t + 1]).then_inc(squared.sem, 1)
                root(root_number(b, hh))
                if not last:
                    make_decays(hh + 1, hd + 1)
                for j in range(2):
                    act.wait_ge(oT_done.sem, oT_done.after(hd, j + 1))
                    act.nop(nofuse=True)
                    split_hi(act_hi[:, bass.ds(2 * hh + j, 1), :].rearrange("p a l -> p (a l)"), ps[:, 6 + j, :])\
                        .then_inc(oT_hi.sem, 1)

            for sig in (*out_stored, silu_done, r_silu):
                sig.open(act)
            load_x(0, 0)
            load_x(0, 1)
            for dst, src in ((g_mix, norm_mix_g), (g_ffn, norm_ffn_g), (g_gla, gla_norm_g),
                             (g_fin, final_norm_g.rearrange("(a n) -> a n", a=1))):
                act.dma_start(dst[:, :], src.to_broadcast([P, src.shape[1]])).then_inc(consts_loaded.sem, 16)
            act.dma_start(wa_raw[:, :, :], a_w).then_inc(consts_loaded.sem, 16)
            act.dma_start(wa2[:, :], w_a2[0]).then_inc(consts_loaded.sem, 16)
            with nc.allow_non_contiguous_dma(reason="512 numbers, once"):
                act.dma_start(b_gate[:, :], b_a[0].rearrange("(h p) -> p h", p=P)).then_inc(consts_loaded.sem, 16)
            load_h(0)
            act.wait_ge(consts_loaded.sem, consts_loaded.after(0, 7))
            act.wait_ge(dve_init.sem, dve_init.after(0, 1))
            look_ahead(FIRST, 0)
            copy_low_rank(0)

            with act.Fori(0, NB) as b:
                first = b * ROUNDS
                for hd in range(H):
                    act.wait_ge(z_done.sem, z_done.after(b, hd + 1))
                    act.activation(softlog[:, hd, :], ps[:, 4 + hd, :], ACT.Abs, bias=b_gate[:, hd:hd + 1])\
                        .then_inc(z_abs.sem, 1)
                act.wait_ge(z_abs.sem, z_abs.after(b, H))
                act.activation(softlog[:, :, :], softlog[:, :, :], ACT.Exp, scale=-1.0).then_inc(z_exp.sem, 1)
                act.wait_ge(z_exp.sem, z_exp.after(b, 1))
                act.activation(softlog[:, :, :], softlog[:, :, :], ACT.Ln, bias=1.0).then_inc(z_log.sem, 1)
                ends = lc[:, :, :].rearrange("p h (t c l) -> p h t c l", c=2, l=CHUNK)[:, :, :, :, CHUNK - 1]
                act.wait_ge(z_scan.sem, z_scan.after(b, H))
                act.wait_ge(odd_kept.sem, odd_kept.after(b, 1))
                act.activation(e_even[:, :, :], ends[:, :, :, 0], ACT.Exp, scale=1 / TAU).then_inc(ends_done.sem, 1)
                act.activation(e_odd[:, :, 1:], ends[:, :, :, 1], ACT.Exp, scale=1 / TAU).then_inc(ends_done.sem, 1)
                act.wait_ge(lc_ready.sem, lc_ready.after(b, 1))

                make_decays(0, b * H)
                with act.Fori(0, H - 1) as hh:
                    head(b, hh, b * H + hh, first + hh * (PAIRS_HEAD // 2), False)
                head(b, H - 1, b * H + (H - 1), first + (H - 1) * (PAIRS_HEAD // 2), True)

                at = passes(b, FFN)
                for step, t in (("square", 0), ("square", 1), ("root", 0), ("square", 2), ("root", 1), ("split", 0),
                                ("square", 3), ("root", 2), ("split", 1), ("root", 3), ("split", 2), ("split", 3)):
                    if step == "square":
                        act.wait_ge(wo_added.sem, wo_added.after(b, NT + t + 1))
                        square(at, t, h[:, t, :])
                    elif step == "root":
                        tile_root(at, t)
                    else:
                        turned_hi(at, t, 0)
                load_x(next_rows(b), 0)
                load_x(next_rows(b), 1)

                c0 = 0
                for (gate, _), size, (up_at, _) in zip(gate_up_banks, GROUPS, group_round):
                    with act.Fori(0, size) as c:
                        chunk = b * NCH + c + c0
                        i = first + c + up_at
                        act.wait_ge(unit_used[1].sem, unit_used[1].after(i, 1))
                        act.wait_ge(prod_done.sem, prod_done.after(chunk))
                        act.activation(silu[:, :], ps[:, gate, :], ACT.Silu).then_inc(silu_done.sem, 1)
                        act.wait_ge(prod_done.sem, prod_done.after(chunk, 1))
                        act.nop(nofuse=True)
                        split_hi(act_hi[:, bass.ds(c, 1), :].rearrange("p a l -> p (a l)"), prod[:, :])\
                            .then_inc(hid_hi.sem, 1)
                    c0 += size

                look_ahead(passes(b, AHEAD), next_rows(b))
                at = passes(b, FINAL)
                for step, t in (("square", 0), ("square", 1), ("root", 0), ("square", 2), ("root", 1), ("store", 0),
                                ("square", 3), ("low rank", 0), ("root", 2), ("store", 1), ("root", 3), ("store", 2), ("store", 3)):
                    if step == "square":
                        act.wait_ge(down_added.sem, down_added.after(b, 3 * NT + t + 1))
                        square(at, t, h[:, t, :])
                    elif step == "root":
                        tile_root(at, t)
                    elif step == "low rank":
                        copy_low_rank(b + 1)
                    else:
                        act.wait_ge(xs_ready.sem, xs_ready.after(at["xs"], t + 1))
                        act.dma_start(out_tok[bass.ds(b * T + t * P, P), :], xs[:, t % 2, :])\
                            .then_inc(out_stored[t % 2].sem, 16)
                load_h(next_rows(b))
            for stored in out_stored:
                act.wait_ge(stored.sem, stored.after(NB))
            for loaded in h_loaded:
                act.wait_ge(loaded.sem, loaded.after(NB, 1))

        @block.vector
        def _(dve):
            def split_lo(dst, src, hi):
                return dve.tensor_tensor(dst, src, hi.bitcast(F32), ALU.subtract)

            def variance_of(n, size, passed, events, cols=slice(0, NT)):
                dve.wait_ge(squared.sem, squared.after(passed, events))
                dve.tensor_scalar(variance[:, cols], sumsq[:, cols], 1 / size, EPS, ALU.mult, ALU.add)\
                    .then_inc(variance_done.sem, 1)

            def root(n, cols=slice(0, NT)):
                dve.wait_ge(root_guess.sem, root_guess.after(n, 1))
                dve.reciprocal(rstd[:, cols], rstd[:, cols]).then_inc(newton_done.sem, 1)
                dve.wait_ge(newton_done.sem, newton_done.after(n, 1))
                dve.tensor_tensor(newton[:, cols], rstd[:, cols], rstd[:, cols], ALU.mult)\
                    .then_inc(newton_done.sem, 1)
                dve.wait_ge(newton_done.sem, newton_done.after(n, 2))
                dve.scalar_tensor_tensor(out=newton[:, cols], in0=newton[:, cols], scalar=-0.5, in1=variance[:, cols],
                                         op0=ALU.mult, op1=ALU.mult).then_inc(newton_done.sem, 1)
                dve.wait_ge(newton_done.sem, newton_done.after(n, 3))
                dve.scalar_tensor_tensor(out=rstd[:, cols], in0=newton[:, cols], scalar=1.5, in1=rstd[:, cols],
                                         op0=ALU.add, op1=ALU.mult).then_inc(rstd_ready.sem, 1)
                dve.wait_ge(rstd_ready.sem, rstd_ready.after(n, 1))

            def tile_variance(at, t):
                variance_of(at["roots"] + t, D, at["squares"], t + 1, slice(t, t + 1))

            def scale(at, t, tile, g):
                root(at["roots"] + t, slice(t, t + 1))
                dve.scalar_tensor_tensor(out=xs[:, t % 2, :], in0=tile, scalar=rstd[:, t:t + 1], in1=g[:, :],
                                         op0=ALU.mult, op1=ALU.mult).then_inc(xs_ready.sem, 1)

            def turned_lo(at, t, bank0):
                for j in range(2):
                    dve.wait_ge(xT_hi_done.sem, xT_hi_done.after(at["turn"], 2 * t + j + 1))
                    blk = (slice(None), slice(4 * j, 4 * j + 4), slice(t * P, (t + 1) * P))
                    split_lo(xT_lo[blk], ps[:, bank0 + 2 * (t % 2) + j, :].rearrange("p (k n) -> p k n", n=P),
                             xT_hi[blk]).then_inc(xT_lo_done.sem, 1)

            def look_ahead_two(at):
                for t in range(2):
                    tile_variance(at, t)
                    scale(at, t, xs[:, t, :], g_mix)

            def look_ahead_rest(at):
                turned_lo(at, 0, 4)
                turned_lo(at, 1, 4)
                for t in (2, 3):
                    tile_variance(at, t)
                    scale(at, t, xs[:, t % 2, :], g_mix)
                    turned_lo(at, t, 4)

            def add_tile(b, done, n, last_unit, last_round, half, bank0, t, added):
                if t < NT - 1:
                    dve.wait_ge(done.sem, done.after(b, n + t + 1))
                else:
                    dve.wait_ge(unit_used[last_unit].sem, unit_used[last_unit].after(last_round, 1))
                part = h[:, t, half * HALF:(half + 1) * HALF]
                dve.tensor_tensor(part, part, ps[:, bank0 + t, :], ALU.add).then_inc(added.sem, 1)

            def scale_qk(hd, i):
                dve.wait_ge(decays.sem, decays.after(hd, 2))
                dve.wait_ge(o_done.sem, o_done.after(hd))
                dve.wait_ge(unit_used[1].sem, unit_used[1].after(i, 1))
                dve.scalar_tensor_tensor(out=qf, in0=ps[:, 0, :], scalar=DK ** -0.5, in1=ef[:, :], op0=ALU.mult,
                                         op1=ALU.mult).then_inc(q_scaled.sem, 1)
                dve.scalar_tensor_tensor(out=qb, in0=ps[:, 0, :], scalar=DK ** -0.5, in1=ei[:, :], op0=ALU.mult,
                                         op1=ALU.mult).then_inc(q_scaled.sem, 1)
                dve.wait_ge(unit_used[3].sem, unit_used[3].after(i, 1))
                dve.tensor_tensor(kf, ps[:, 1, :], ei[:, :], ALU.mult).then_inc(k_scaled.sem, 1)
                dve.tensor_tensor(kb, ps[:, 1, :], ef[:, :], ALU.mult).then_inc(k_scaled.sem, 1)

            def gate_r(hh, hd):
                dve.wait_ge(r_silu.sem, r_silu.after(hd, 1))
                dve.tensor_tensor(r_gate[:, :, :], r_gate[:, :, :],
                                  g_gla[:, bass.ds(hh * DV, DV)].unsqueeze(1).to_broadcast([P, NT, DV]),
                                  ALU.mult).then_inc(r_done.sem, 1)

            def head(b, hh, hd, i, last):
                dve.wait_ge(future_done.sem, future_done.after(hd, 1))
                dve.wait_ge(past_copied.sem, past_copied.after(hd, 2))
                dve.nop(nofuse=True)
                back = ps[:, 7, :].rearrange("p (t n) -> p t n", n=P)
                for c in range(2):
                    part = (slice(c * CHUNK, (c + 1) * CHUNK), slice(None), slice(c * CHUNK, (c + 1) * CHUNK))
                    dve.copy_predicated(scores[part], future[c * CHUNK:(c + 1) * CHUNK, :, :], back[part])\
                        .then_inc(scores_ready.sem, 1)

                mine = state[:, bass.ds(hh, 1), :].rearrange("p a v -> p (a v)")
                for t in range(NT):
                    if t > 0:
                        dve.wait_ge(state_done.sem, state_done.after(hd, t))
                    dve.tensor_scalar(state_in[:, t, :], mine,
                                      e_odd[:, bass.ds(hh, 1), t:t + 1].rearrange("p a t -> p (a t)"),
                                      e_even[:, bass.ds(hh, 1), t:t + 1].rearrange("p a t -> p (a t)"), ALU.mult,
                                      ALU.mult).then_inc(state_in_done.sem, 1)
                    if t == 0 and not last:
                        gate_r(hh, hd)
                    dve.wait_ge(state_in_done.sem, state_in_done.after(hd, t + 1))
                    dve.wait_ge(ds_done.sem, ds_done.after(hd, 2 * (t // 2) + 2))
                    dve.tensor_tensor(mine, state_in[:, t, :], ps[:, 1, (t % 2) * DV:(t % 2 + 1) * DV],
                                      ALU.add).then_inc(state_done.sem, 1)
                if last:
                    gate_r(hh, hd)
                variance_of(root_number(b, hh), DV, squares_pass(b, hh), NT)
                root(root_number(b, hh))
                dve.wait_ge(r_done.sem, r_done.after(hd, 1))
                for t in range(NT):
                    dve.scalar_tensor_tensor(out=og[:, t, :], in0=ps[:, 6 + t // 2, (t % 2) * DV:(t % 2 + 1) * DV],
                                             scalar=rstd[:, t:t + 1], in1=r_gate[:, t, :], op0=ALU.mult,
                                             op1=ALU.mult).then_inc(og_done.sem, 1)
                if not last:
                    scale_qk(hd + 1, i + 3)
                for j in range(2):
                    dve.wait_ge(oT_hi.sem, oT_hi.after(hd, j + 1))
                    split_lo(act_lo[:, bass.ds(2 * hh + j, 1), :].rearrange("p a l -> p (a l)"), ps[:, 6 + j, :],
                             act_hi[:, bass.ds(2 * hh + j, 1), :].rearrange("p a l -> p (a l)"))\
                        .then_inc(oT_lo.sem, 1)

            for sig in (oT_lo, prod_done, k_scaled, hid_lo, down_added):
                sig.open(dve)
            dve.memset(scores[:, :, :], 0.0)
            dve.memset(state[:, :, :], 0.0)
            dve.memset(e_odd[:, :, :], 1.0).then_inc(dve_init.sem, 1)
            dve.wait_ge(dve_init.sem, dve_init.after(0, 1))
            dve.wait_ge(consts_loaded.sem, consts_loaded.after(0, 7))
            dve.wait_ge(masks.sem, masks.after(0, 1))
            look_ahead_two(FIRST)
            look_ahead_rest(FIRST)

            with dve.Fori(0, NB) as b:
                first = b * ROUNDS
                for hd in range(H):
                    dve.wait_ge(z_abs.sem, z_abs.after(b, hd + 1))
                    dve.tensor_scalar(lc[:, hd, :], ps[:, 4 + hd, :], b_gate[:, hd:hd + 1], 0.0, ALU.add, ALU.min)\
                        .then_inc(z_min.sem, 1)
                dve.wait_ge(z_min.sem, z_min.after(b, H))
                dve.wait_ge(z_log.sem, z_log.after(b, 1))
                dve.tensor_tensor(lc[:, :, :], lc[:, :, :], softlog[:, :, :], ALU.subtract).then_inc(z_sub.sem, 1)
                dve.wait_ge(z_sub.sem, z_sub.after(b, 1))
                for hd in range(H):
                    dve.tensor_tensor_scan(lc[:, hd, :], carry_mask[:, :], lc[:, hd, :], 0.0, ALU.mult,
                                           ALU.add).then_inc(z_scan.sem, 1)
                dve.wait_ge(z_scan.sem, z_scan.after(b, H))
                dve.tensor_copy(e_odd[:, :, 0:1], e_odd[:, :, NT:]).then_inc(odd_kept.sem, 1)
                chunks = lc[:, :, :].rearrange("p h (t c l) -> p (h t) c l", c=2, l=CHUNK)
                dve.tensor_copy(lend[:, :], chunks[:, :, 0, CHUNK - 1]).then_inc(lend_done.sem, 1)
                dve.wait_ge(lend_done.sem, lend_done.after(b, 1))
                dve.wait_ge(ends_done.sem, ends_done.after(b, 2))
                dve.tensor_tensor(chunks[:, :, 0, :], chunks[:, :, 0, :],
                                  lend[:, :].unsqueeze(2).to_broadcast([P, H * NT, CHUNK]),
                                  ALU.subtract).then_inc(lc_ready.sem, 1)

                scale_qk(b * H, first)
                with dve.Fori(0, H - 1) as hh:
                    head(b, hh, b * H + hh, first + hh * (PAIRS_HEAD // 2), False)
                head(b, H - 1, b * H + (H - 1), first + (H - 1) * (PAIRS_HEAD // 2), True)

                for t in range(NT):
                    dve.wait_ge(h_loaded[t].sem, h_loaded[t].after(b, 1))
                    add_tile(b, wo_done, 0, 3, first + ROUND_OUT + 1, 0, 0, t, wo_added)
                at = passes(b, FFN)
                for step, t in (("add", 0), ("add", 1), ("variance", 0), ("add", 2), ("scale", 0), ("variance", 1),
                                ("scale", 1), ("add", 3), ("split", 0), ("variance", 2), ("scale", 2), ("split", 1),
                                ("variance", 3), ("scale", 3), ("split", 2), ("split", 3)):
                    if step == "add":
                        add_tile(b, wo_done, NT - 1, 3, first + ROUND_OUT + 3, 1, 4, t, wo_added)
                    elif step == "variance":
                        tile_variance(at, t)
                    elif step == "scale":
                        if t < 2:
                            dve.wait_ge(out_stored[t].sem, out_stored[t].after(b))
                        else:
                            dve.wait_ge(xs_turned.sem, xs_turned.after(at["turn"], t - 1))
                        scale(at, t, h[:, t, :], g_ffn)
                    else:
                        turned_lo(at, t, 0)

                ahead = passes(b, AHEAD)
                c0 = 0
                for g, (size, (up_at, down_at)) in enumerate(zip(GROUPS, group_round)):
                    with dve.Fori(0, size) as c:
                        chunk = b * NCH + c + c0
                        dve.wait_ge(silu_done.sem, silu_done.after(chunk, 1))
                        dve.wait_ge(unit_used[3].sem, unit_used[3].after(first + c + up_at, 1))
                        dve.wait_ge(hid_lo.sem, hid_lo.after(chunk))
                        dve.tensor_tensor(prod[:, :], silu[:, :], ps[:, gate_up_banks[g][1], :], ALU.mult).then_inc(prod_done.sem, 1)
                        dve.wait_ge(hid_hi.sem, hid_hi.after(chunk, 1))
                        split_lo(act_lo[:, bass.ds(c, 1), :].rearrange("p a l -> p (a l)"), prod[:, :],
                                 act_hi[:, bass.ds(c, 1), :].rearrange("p a l -> p (a l)")).then_inc(hid_lo.sem, 1)
                    if g == len(GROUPS) - 1:
                        look_ahead_two(ahead)
                    for half in range(2):
                        n = (half + 1) * size - 1
                        for t in range(NT):
                            add_tile(b, down_done, (2 * g + half) * (NT - 1), n % 4, first + down_at + n // 4, half,
                                     down_bank(g, half), t, down_added)
                        if g == len(GROUPS) - 1 and half == 0:
                            look_ahead_rest(ahead)
                    c0 += size

                at = passes(b, FINAL)
                for t in range(NT):
                    tile_variance(at, t)
                    if t >= 2:
                        dve.wait_ge(out_stored[t % 2].sem, out_stored[t % 2].after(b, 1))
                    else:
                        dve.wait_ge(xs_turned.sem, xs_turned.after(ahead["turn"], NT))
                    scale(at, t, h[:, t, :], g_fin)


_INS = ["x", "norm_mix_g", "norm_ffn_g", "gla_w_in", "gla_w_a2", "gla_b_a", "gla_norm_g", "gla_w_out", "ffn_w_gu",
        "ffn_w_down", "final_norm_g"]


def kernel(**inputs):
    import numpy as np
    import concourse.bacc as bacc
    from concourse.bass_utils import run_bass_kernel_spmd

    nc = bacc.Bacc("TRN2", target_bir_lowering=False, num_devices=1)
    arrays, args = {}, []
    for name in _INS:
        a = np.ascontiguousarray(inputs[name])
        arrays[f"in_{name}"] = a
        args.append(nc.dram_tensor(f"in_{name}", a.shape, mybir.dt.from_np(a.dtype), kind="ExternalInput").ap())
    args.append(nc.dram_tensor("out_0", inputs["x"].shape, F32, kind="ExternalOutput").ap())
    gla_layer(nc, *args)
    return run_bass_kernel_spmd(nc, [arrays], core_ids=[0]).results[0]["out_0"]
```

```python
from contextlib import ExitStack

import concourse.bass as bass
from concourse import mybir

P = 128
F32 = mybir.dt.float32
F32R = mybir.dt.float32r
I32 = mybir.dt.int32
BF16 = mybir.dt.bfloat16
ALU = mybir.AluOpType
ACT = mybir.ActivationFunctionType

CHUNK = 64
EPS = 1e-6
TAU = 16.0


class Signal:

    def __init__(self, sem, per, size=1, opened=False):
        self.sem, self.per, self.size, self.opened = sem, per, size, opened

    def after(self, iteration, n=0):
        return (iteration * self.per + (self.per if self.opened else 0) + n) * self.size

    def open(self, eng):
        assert self.opened
        eng.sem_inc(self.sem, self.per * self.size)


def gla_layer(nc, x, norm_mix_g, norm_ffn_g, w_in, w_a2, b_a, gla_norm_g, w_out, w_gu, w_down, final_norm_g, out):
    _, SEQ, D = x.shape
    RANK, QK = w_a2.shape[1], w_a2.shape[2]
    VD = w_out.shape[1]
    HID = w_down.shape[1]
    DK = P
    H = QK // DK
    DV = VD // H
    T = 512
    NB = SEQ // T
    NT = T // P
    KD = D // P
    KV = VD // P
    NCH = HID // P
    GROUPS = (12, NCH - 12)
    HALF = D // 2
    assert RANK == 16 and T == 4 * P and KD == 8 and KV == 8 and DV == 2 * P and all(g % 2 == 0 for g in GROUPS)

    UNIT = 512
    PAIRS_HEAD = 2 + KD // 2
    PAIRS = H * PAIRS_HEAD + KV + 2 * NCH + NCH
    ROUNDS = PAIRS // 2
    ROUND_OUT = H * PAIRS_HEAD // 2
    assert PAIRS % 2 == 0 and PAIRS_HEAD % 2 == 0
    group_round, at = [], ROUND_OUT + KV // 2
    for g in GROUPS:
        group_round.append((at, at + g))
        at += g + g // 2
    assert at == ROUNDS
    TURN_AFTER = (0, 1, 3, 4)
    LOW_RANK_AFTER, GATES_AFTER = 5, 6

    q_w = w_in[0, :, 0:QK].rearrange("(k p) n -> p k n", p=P)
    k_w = w_in[0, :, QK:2 * QK].rearrange("(k p) n -> p k n", p=P)
    v_w = w_in[0, :, 2 * QK:2 * QK + VD].rearrange("(k p) n -> p k n", p=P)
    r_w = w_in[0, :, 2 * QK + VD:2 * QK + 2 * VD].rearrange("(k p) n -> p k n", p=P)
    a_w = w_in[0, :, 2 * QK + 2 * VD:].rearrange("(k p) n -> p k n", p=P)
    o_w = w_out[0].rearrange("(k p) n -> p k n", p=P)
    gu_w = w_gu[0].rearrange("(k p) n -> p k n", p=P)
    d_w = w_down[0].rearrange("(k p) n -> p k n", p=P)
    x_tok = x[0]
    out_tok = out[0]

    with ExitStack() as ctx:
        def sb(name, shape, dt=F32):
            return ctx.enter_context(nc.sbuf_tensor(name, shape, dt))

        def signal(name, per=1, size=1, opened=False):
            return Signal(ctx.enter_context(nc.semaphore(name)), per, size, opened)

        ident = sb("ident", [P, P])
        future = sb("future", [P, NT, CHUNK], I32)
        carry_mask = sb("carry_mask", [P, T])
        g_mix = sb("g_mix", [P, D])
        g_ffn = sb("g_ffn", [P, D])
        g_fin = sb("g_fin", [P, D])
        g_gla = sb("g_gla", [P, VD])
        b_gate = sb("b_gate", [P, H])
        wa2_raw = sb("wa2_raw", [6 * RANK, QK])
        wa2_parts = sb("wa2_parts", [6 * RANK, QK], F32R)
        wa_raw = sb("wa_raw", [P, KD, RANK])
        wa_for_hi = sb("wa_for_hi", [P, KD, 6 * RANK], F32R)
        wa_for_lo = sb("wa_for_lo", [P, KD, 6 * RANK], F32R)
        h = sb("h", [P, NT, D])
        xs = sb("xs", [P, 2, D])
        junk = sb("junk", [P, D], BF16)
        sumsq = sb("sumsq", [P, NT])
        rstd = sb("rstd", [P, NT])
        variance = sb("variance", [P, NT])
        newton = sb("newton", [P, NT])
        xT_hi = sb("xT_hi", [P, KD, T], F32R)
        xT_lo = sb("xT_lo", [P, KD, T], F32R)
        act_hi = sb("act_hi", [P, max(GROUPS), T], F32R)
        act_lo = sb("act_lo", [P, max(GROUPS), T], F32R)
        raw = sb("raw", [P, 2, 2, UNIT])
        ring_hi = sb("ring_hi", [P, 4, UNIT], F32R)
        ring_lo = sb("ring_lo", [P, 4, UNIT], F32R)
        aT = sb("aT", [6 * RANK, T], F32R)
        lc = sb("lc", [P, H, T])
        lend = sb("lend", [P, H * NT])
        e_even = sb("e_even", [P, H, NT])
        e_odd = sb("e_odd", [P, H, NT + 1])
        ef = sb("ef", [P, T])
        ei = sb("ei", [P, T])
        qk_scaled = sb("qk_scaled", [P, 4, T])
        qf, qb, kf, kb = (qk_scaled[:, n, :] for n in range(4))
        k_hi = sb("k_hi", [P, T], F32R)
        v_hi = sb("v_hi", [P, NT, DV], F32R)
        r_gate = sb("r_gate", [P, NT, DV])
        scores = sb("scores", [P, NT, P])
        state = sb("state", [P, H, DV])
        state_in = sb("state_in", [P, NT, DV])
        og = sb("og", [P, NT, DV])
        k_lo = act_lo[:, KV, :]
        v_lo = act_lo[:, KV + 1:KV + 3, :].rearrange("p a (t v) -> p (a t) v", v=DV)
        scores_hi = act_hi[:, KV, :].rearrange("p (t q) -> p t q", q=P)
        scores_lo = act_lo[:, KV + 3, :].rearrange("p (t q) -> p t q", q=P)
        silu, prod = ef, ei
        out_tiles = [xs[:, 0, :], xs[:, 1, :], og[:, :, :].rearrange("p t v -> p (t v)"),
                     r_gate[:, :, :].rearrange("p t v -> p (t v)")]
        softlog = qk_scaled

        ps = ctx.enter_context(nc.psum_tensor("ps", [P, 8, UNIT], F32))

        mix_loaded = signal("mix_loaded", 1, 16)
        wa_loaded = signal("wa_loaded", 1, 16)
        wa2_loaded = signal("wa2_loaded", 6, 16)
        b_loaded = signal("b_loaded", 1, 16)
        norms_loaded = signal("norms_loaded", 3, 16)
        first_loaded = [signal(f"first_loaded{i}", 1, 16) for i in range(NT)]
        masks = signal("masks")
        wa_ready = signal("wa_ready")
        pool_init = signal("pool_init")
        dve_init = signal("dve_init")
        raw_loaded = [signal(f"raw_loaded{i}", 1, 32) for i in range(2)]
        unit_hi = [signal(f"unit_hi{i}") for i in range(4)]
        unit_split = [signal(f"unit_split{i}", opened=True) for i in range(4)]
        unit_used = [signal(f"unit_used{i}", opened=True) for i in range(4)]
        x_in = [signal(f"x_in{i}", NT // 2, 16) for i in range(2)]
        h_loaded = [signal(f"h_loaded{i}", 1, 16) for i in range(NT)]
        squared = signal("squared", NT)
        variance_done = signal("variance_done")
        root_guess = signal("root_guess")
        newton_done = signal("newton_done", 3)
        rstd_ready = signal("rstd_ready")
        xs_ready = signal("xs_ready", NT)
        xs_turned = signal("xs_turned", NT)
        xT_hi_done = signal("xT_hi_done", 2 * NT)
        xT_lo_done = signal("xT_lo_done", 2 * NT)
        out_stored = [signal(f"out_stored{i}", NT // 2, 16, opened=True) for i in range(2)]
        a_done = signal("a_done")
        aT_hi_done = signal("aT_hi_done")
        aT_done = signal("aT_done")
        z_done = signal("z_done", H)
        z_abs = signal("z_abs", H)
        z_min = signal("z_min", H)
        z_exp = signal("z_exp")
        z_log = signal("z_log")
        z_sub = signal("z_sub")
        z_scan = signal("z_scan", H)
        odd_kept = signal("odd_kept")
        lend_done = signal("lend_done")
        ends_done = signal("ends_done", 2)
        lc_ready = signal("lc_ready")
        decays = signal("decays", 2)
        q_scaled = signal("q_scaled", 2)
        k_scaled = signal("k_scaled", 2, opened=True)
        vr_done = signal("vr_done", NT - 1)
        v_hi_done = signal("v_hi_done", 2)
        v_done = signal("v_done", 2)
        r_silu = signal("r_silu", opened=True)
        r_done = signal("r_done")
        kt_done = signal("kt_done")
        k_hi_done = signal("k_hi_done")
        k_tok_done = signal("k_tok_done")
        past_done = signal("past_done")
        future_done = signal("future_done")
        past_copied = signal("past_copied", 2)
        scores_ready = signal("scores_ready", 2)
        scores_hi_done = signal("scores_hi_done")
        scores_split = signal("scores_split")
        ds_done = signal("ds_done", NT)
        state_in_done = signal("state_in_done", NT)
        state_done = signal("state_done", NT)
        o_done = signal("o_done", NT, opened=True)
        og_done = signal("og_done", NT)
        oT_done = signal("oT_done", 2)
        oT_hi = signal("oT_hi", 2)
        oT_lo = signal("oT_lo", 2, opened=True)
        wo_done = signal("wo_done", 2 * (NT - 1))
        wo_added = signal("wo_added", 2 * NT)
        silu_done = signal("silu_done", opened=True)
        prod_done = signal("prod_done", opened=True)
        hid_hi = signal("hid_hi")
        hid_lo = signal("hid_lo", opened=True)
        down_done = signal("down_done", 4 * (NT - 1))
        down_added = signal("down_added", 4 * NT, opened=True)

        FFN, AHEAD, FINAL = H, H + 1, H + 2
        ROOTS = H + (NT - 1) + NT + 1

        def squares_pass(b, n):
            return b * (H + 3) + (n + 1)

        def root_number(b, n):
            in_block = n
            if not isinstance(n, bass.RuntimeValue) and n > FFN:
                in_block = H + NT - 1 + (NT if n == FINAL else 0)
            return b * ROOTS + NT - 1 + in_block

        def xs_pass(b, n):
            return b * 3 + (n - H + 1)

        def turn_pass(b, n):
            return b * 2 + (n - H + 1)

        def next_rows(b):
            return ((b + 1) % NB) * T

        gate_up_banks = ((4, 5), (0, 1))

        def down_bank(g, half):
            return 4 * ((g + half) % 2)

        FIRST = dict(squares=0, roots=0, xs=0, turn=0, block=0)

        def passes(b, n):
            return dict(squares=squares_pass(b, n), roots=root_number(b, n), xs=xs_pass(b, n),
                        turn=turn_pass(b, n) if n != FINAL else None, block=b + 1)

        block = ctx.enter_context(nc.Block())

        @block.sync
        def _(sp):
            def load_pair(i, p, parts):
                sp.wait_ge(unit_split[2 * p].sem, unit_split[2 * p].after(i))
                sp.wait_ge(unit_split[2 * p + 1].sem, unit_split[2 * p + 1].after(i))
                for dst, src in parts:
                    sp.dma_start(dst, src).then_inc(raw_loaded[p].sem, 16)

            def columns(i, p, w, start):
                load_pair(i, p, [(raw[:, p, u, :].rearrange("p (k n) -> p k n", k=4),
                                  w[:, 4 * u:4 * u + 4, bass.ds(start, P)]) for u in range(2)])

            def rows(i, p, w, k, start):
                load_pair(i, p, [(raw[:, p, u, :], w[:, k + u, start:start + UNIT]) for u in range(2)])

            def qk(i, hd):
                columns(i, 0, q_w, hd * DK)
                columns(i, 1, k_w, hd * DK)

            def vr(i, hd):
                for n in range(2):
                    for p in range(2):
                        k = 4 * n + 2 * p
                        load_pair(i + n, p, [(raw[:, p, :, 0:DV], v_w[:, k:k + 2, bass.ds(hd * DV, DV)]),
                                             (raw[:, p, :, DV:], r_w[:, k:k + 2, bass.ds(hd * DV, DV)])])

            for t in range(NT):
                sp.dma_start(h[:, t, :], x_tok[t * P:(t + 1) * P, :]).then_inc(first_loaded[t].sem, 16)
            for part in range(6):
                sp.dma_start(wa2_raw[part * RANK:(part + 1) * RANK, :], w_a2[0]).then_inc(wa2_loaded.sem, 16)
            for dst, src in ((g_ffn, norm_ffn_g), (g_gla, gla_norm_g),
                             (g_fin, final_norm_g.rearrange("(a n) -> a n", a=1))):
                sp.dma_start(dst[:, :], src.to_broadcast([P, src.shape[1]])).then_inc(norms_loaded.sem, 16)
            with sp.Fori(0, NB) as b:
                first = b * ROUNDS
                qk(first, 0)
                with sp.Fori(0, H - 1) as hd:
                    vr(first + hd * (PAIRS_HEAD // 2) + 1, hd)
                    qk(first + hd * (PAIRS_HEAD // 2) + 3, hd + 1)
                vr(first + ROUND_OUT - 2, H - 1)
                for n in range(KV):
                    half, k2 = divmod(n, KV // 2)
                    rows(first + ROUND_OUT + n // 2, n % 2, o_w, 2 * k2, half * HALF)
                c0 = 0
                for size, (up_at, down_at) in zip(GROUPS, group_round):
                    with sp.Fori(0, size) as c:
                        columns(first + c + up_at, 0, gu_w, c * P + c0 * P)
                        columns(first + c + up_at, 1, gu_w, c * P + (c0 * P + HID))
                    for n in range(size):
                        half, k2 = divmod(n, size // 2)
                        rows(first + down_at + n // 2, n % 2, d_w, c0 + 2 * k2, half * HALF)
                    c0 += size

        @block.gpsimd
        def _(pool):
            def step(ins):
                pool_steps[0] += 1
                ins.then_inc(pool_init.sem, 1)
                pool.wait_ge(pool_init.sem, pool_steps[0])

            for split in unit_split:
                split.open(pool)
            pool_steps = [0]
            step(pool.memset(ident[:, :], 0.0))
            step(pool.memset(future[:, :, :], 1))
            step(pool.memset(carry_mask[:, :], 1.0))
            step(pool.memset(wa_for_hi[:, :, :].bitcast(F32), 0.0))
            step(pool.memset(wa_for_lo[:, :, :].bitcast(F32), 0.0))
            step(pool.affine_select(out=ident[:, :], in_=ident[:, :], compare_op=ALU.not_equal, fill=1.0,
                                    base=0, pattern=[[-1, P]], channel_multiplier=1))
            for half in range(2):
                rows_ = future[half * CHUNK:(half + 1) * CHUNK, :, :]
                step(pool.affine_select(out=rows_, in_=rows_, compare_op=ALU.is_gt, fill=0.0, base=0,
                                        pattern=[[0, NT], [-1, CHUNK]], channel_multiplier=1))
            pool.memset(carry_mask[:, :].rearrange("p (c l) -> p c l", l=CHUNK)[:, :, 0:1], 0.0).then_inc(masks.sem, 1)
            pool.wait_ge(wa_loaded.sem, wa_loaded.after(0, 1))
            for part in range(3):
                hi = slice(2 * part * RANK, (2 * part + 1) * RANK)
                lo = slice((2 * part + 1) * RANK, (2 * part + 2) * RANK)
                step(pool.tensor_copy(wa_for_lo[:, :, hi], wa_raw[:, :, :]))
                step(pool.tensor_copy(wa_for_hi[:, :, hi], wa_raw[:, :, :]))
                step(pool.tensor_tensor(wa_for_hi[:, :, lo], wa_raw[:, :, :], wa_for_hi[:, :, hi].bitcast(F32),
                                        ALU.subtract))
            pool.wait_ge(wa2_loaded.sem, wa2_loaded.after(0, 6))
            step(pool.tensor_copy(wa2_parts[:, :], wa2_raw[:, :]))
            mid = slice(2 * RANK, 4 * RANK)
            pool.tensor_tensor(wa2_parts[mid, :], wa2_raw[mid, :], wa2_parts[mid, :].bitcast(F32),
                               ALU.subtract).then_inc(wa_ready.sem, 1)
            pool.wait_ge(wa_ready.sem, wa_ready.after(0, 1))

            with pool.Fori(0, NB * ROUNDS) as i:
                for u in range(4):
                    p = u // 2
                    if u % 2 == 0:
                        pool.wait_ge(raw_loaded[p].sem, raw_loaded[p].after(i, 1))
                    pool.wait_ge(unit_used[u].sem, unit_used[u].after(i))
                    pool.nop(nofuse=True)
                    pool.tensor_scalar(ring_hi[:, u, :], raw[:, p, u % 2, :], 1.0, 0.0, ALU.mult,
                                       ALU.add).then_inc(unit_hi[u].sem, 1)
                    pool.wait_ge(unit_hi[u].sem, unit_hi[u].after(i, 1))
                    pool.tensor_tensor(ring_lo[:, u, :], raw[:, p, u % 2, :], ring_hi[:, u, :].bitcast(F32),
                                       ALU.subtract).then_inc(unit_split[u].sem, 1)

        @block.tensor
        def _(pe):
            def three(out, l_hi, l_lo, r_hi, r_lo, first, last):
                pe.matmul(out, l_hi, r_hi, start=first, stop=False)
                pe.matmul(out, l_hi, r_lo, start=False, stop=False)
                return pe.matmul(out, l_lo, r_hi, start=False, stop=last)

            def column_units(i, p, out):
                for k in range(KD):
                    u = 2 * p + k // 4
                    if k % 4 == 0:
                        pe.wait_ge(unit_split[u].sem, unit_split[u].after(i, 1))
                    cols = slice((k % 4) * P, (k % 4 + 1) * P)
                    ins = three(out, ring_hi[:, u, cols], ring_lo[:, u, cols], xT_hi[:, k, :], xT_lo[:, k, :],
                                k == 0, k == KD - 1)
                    if k % 4 == 3:
                        ins.then_inc(unit_used[u].sem, 1)

            def half_column_units(i, p, bank, tokens):
                tok = slice(tokens * T // 2, (tokens + 1) * T // 2)
                for k in range(KD):
                    u = 2 * p + k // 4
                    if k % 4 == 0 and tokens == 0:
                        pe.wait_ge(unit_split[u].sem, unit_split[u].after(i, 1))
                    cols = slice((k % 4) * P, (k % 4 + 1) * P)
                    ins = three(ps[:, bank, tok], ring_hi[:, u, cols], ring_lo[:, u, cols], xT_hi[:, k, tok],
                                xT_lo[:, k, tok], k == 0, k == KD - 1)
                    if k % 4 == 3 and tokens == 1:
                        ins.then_inc(unit_used[u].sem, 1)

            def row_unit(i, u, l_hi, l_lo, k, bank0, first, last, done=None):
                pe.wait_ge(unit_split[u].sem, unit_split[u].after(i, 1))
                for t in range(NT):
                    tok = slice(t * P, (t + 1) * P)
                    ins = three(ps[:, bank0 + t, :], l_hi[:, k, tok], l_lo[:, k, tok], ring_hi[:, u, :],
                                ring_lo[:, u, :], first, last)
                    if last and done is not None and t < NT - 1:
                        ins.then_inc(done.sem, 1)
                ins.then_inc(unit_used[u].sem, 1)

            def turn_tile(at, t, bank0):
                pe.wait_ge(xs_ready.sem, xs_ready.after(at["xs"], t + 1))
                if t >= 2:
                    pe.wait_ge(xT_lo_done.sem, xT_lo_done.after(at["turn"], 2 * (t - 1)))
                for k in range(KD):
                    ins = pe.transpose(ps[:, bank0 + 2 * (t % 2) + k // 4, (k % 4) * P:(k % 4 + 1) * P],
                                       xs[:, t % 2, k * P:(k + 1) * P], ident[:, :])
                ins.then_inc(xs_turned.sem, 1)

            def low_rank(at):
                pe.wait_ge(xT_lo_done.sem, xT_lo_done.after(at["turn"], 2 * NT))
                for k in range(KD):
                    pe.matmul(ps[0:6 * RANK, 6, :], wa_for_hi[:, k, :], xT_hi[:, k, :], start=k == 0, stop=False)
                    ins = pe.matmul(ps[0:6 * RANK, 6, :], wa_for_lo[:, k, :], xT_lo[:, k, :], start=False,
                                    stop=k == KD - 1)
                ins.then_inc(a_done.sem, 1)

            def gates(at):
                pe.wait_ge(aT_done.sem, aT_done.after(at["block"], 1))
                for hd in range(H):
                    pe.matmul(ps[:, 4 + hd, :], wa2_parts[:, hd * DK:(hd + 1) * DK], aT[:, :], start=True,
                              stop=True).then_inc(z_done.sem, 1)

            def vr_units(i, n, units):
                for u in units:
                    row_unit(i, u, xT_hi, xT_lo, 4 * n + u, 2, n + u == 0, n == 1 and u == 3, vr_done)

            def make_scores(hd):
                pe.wait_ge(k_scaled.sem, k_scaled.after(hd, 2))
                for t in range(NT):
                    tok = slice(t * P, (t + 1) * P)
                    ins = pe.transpose(ps[:, 0, tok], kf[:, tok], ident[:, :])
                ins.then_inc(kt_done.sem, 1)
                pe.wait_ge(oT_lo.sem, oT_lo.after(hd))
                for t in range(NT):
                    tok = slice(t * P, (t + 1) * P)
                    ins = pe.matmul(ps[:, 6, tok], kf[:, tok], qf[:, tok], start=True, stop=True)
                ins.then_inc(past_done.sem, 1)
                for t in range(NT):
                    tok = slice(t * P, (t + 1) * P)
                    ins = pe.matmul(ps[:, 7, tok], kb[:, tok], qb[:, tok], start=True, stop=True)
                ins.then_inc(future_done.sem, 1)

            def use_scores(hd, meanwhile=None):
                for two in range(2):
                    pe.wait_ge(v_done.sem, v_done.after(hd, two + 1))
                    if two == 0:
                        pe.wait_ge(k_tok_done.sem, k_tok_done.after(hd, 1))
                    else:
                        pe.wait_ge(state_done.sem, state_done.after(hd, 2))
                    for t in (2 * two, 2 * two + 1):
                        three(ps[:, 1, (t % 2) * DV:(t % 2 + 1) * DV], k_hi[:, t * P:(t + 1) * P],
                              k_lo[:, t * P:(t + 1) * P], v_hi[:, t, :], v_lo[:, t, :], True,
                              True).then_inc(ds_done.sem, 1)
                    if two == 0:
                        pe.wait_ge(scores_split.sem, scores_split.after(hd, 1))
                    for t in (2 * two, 2 * two + 1):
                        o = ps[:, 6 + two, (t % 2) * DV:(t % 2 + 1) * DV]
                        three(o, scores_hi[:, t, :], scores_lo[:, t, :], v_hi[:, t, :], v_lo[:, t, :], True, False)
                        if t % 2 == 1 and meanwhile is not None:
                            meanwhile(two)
                        pe.wait_ge(state_in_done.sem, state_in_done.after(hd, t + 1))
                        pe.matmul(o, qf[:, t * P:(t + 1) * P], state_in[:, t, :], start=False,
                                  stop=True).then_inc(o_done.sem, 1)

            def turn_o(hd):
                pe.wait_ge(og_done.sem, og_done.after(hd, NT))
                for j in range(2):
                    for t in range(NT):
                        ins = pe.transpose(ps[:, 6 + j, t * P:(t + 1) * P], og[:, t, j * P:(j + 1) * P], ident[:, :])
                    ins.then_inc(oT_done.sem, 1)

            for sig in (*unit_used, o_done):
                sig.open(pe)
            pe.wait_ge(masks.sem, masks.after(0, 1))
            for t in range(NT):
                turn_tile(FIRST, t, 4)
            pe.wait_ge(wa_ready.sem, wa_ready.after(0, 1))
            low_rank(FIRST)
            gates(FIRST)

            with pe.Fori(0, NB) as b:
                first = b * ROUNDS
                pe.wait_ge(down_added.sem, down_added.after(b, 1 - NT))
                column_units(first, 0, ps[:, 0, :])
                pe.wait_ge(down_added.sem, down_added.after(b))
                column_units(first, 1, ps[:, 1, :])
                pe.wait_ge(z_min.sem, z_min.after(b, H))
                pe.wait_ge(r_silu.sem, r_silu.after(b * H))
                vr_units(first + 1, 0, range(4))

                with pe.Fori(0, H - 1) as hh:
                    hd = b * H + hh
                    i = first + hh * (PAIRS_HEAD // 2)
                    make_scores(hd)
                    vr_units(i + 2, 1, range(4))
                    pe.wait_ge(k_tok_done.sem, k_tok_done.after(hd, 1))
                    column_units(i + 3, 0, ps[:, 0, :])
                    pe.wait_ge(r_silu.sem, r_silu.after(hd, 1))
                    use_scores(hd, lambda two: vr_units(i + 4, 0, (two,)))
                    pe.wait_ge(state_done.sem, state_done.after(hd, NT))
                    column_units(i + 3, 1, ps[:, 1, :])
                    vr_units(i + 4, 0, (2,))
                    turn_o(hd)
                    vr_units(i + 4, 0, (3,))
                last = b * H + (H - 1)
                make_scores(last)
                vr_units(first + ROUND_OUT - 1, 1, range(4))
                use_scores(last)

                pe.wait_ge(state_done.sem, state_done.after(last, NT))
                pe.wait_ge(r_silu.sem, r_silu.after(last, 1))
                pe.wait_ge(oT_lo.sem, oT_lo.after(last))
                for n in range(KV + 4):
                    half, k = divmod(n, KV)
                    if n == KV - 4:
                        turn_o(last)
                    if n == KV - 2:
                        pe.wait_ge(oT_lo.sem, oT_lo.after(last, 2))
                    row_unit(first + ROUND_OUT + n // 4, n % 4, act_hi, act_lo, k, 4 * half, k == 0, k == KV - 1,
                             wo_done)
                i = first + ROUND_OUT + 3
                at = passes(b, FFN)
                for t in range(NT):
                    if t == NT - 1:
                        turn_tile(at, 0, 0)
                    tok = slice(t * P, (t + 1) * P)
                    for u in range(4):
                        if t == 0:
                            pe.wait_ge(unit_split[u].sem, unit_split[u].after(i, 1))
                        ins = three(ps[:, 4 + t, :], act_hi[:, 4 + u, tok], act_lo[:, 4 + u, tok], ring_hi[:, u, :],
                                    ring_lo[:, u, :], False, u == 3)
                        if t == NT - 1:
                            ins.then_inc(unit_used[u].sem, 1)
                    if t < NT - 1:
                        ins.then_inc(wo_done.sem, 1)

                i = first + group_round[0][0]
                turn_tile(at, 1, 0)
                pe.wait_ge(xT_lo_done.sem, xT_lo_done.after(at["turn"], 4))
                half_column_units(i, 0, 4, 0)
                turn_tile(at, 2, 0)
                turn_tile(at, 3, 0)
                half_column_units(i, 1, 5, 0)
                pe.wait_ge(xT_lo_done.sem, xT_lo_done.after(at["turn"], 8))
                half_column_units(i, 0, 4, 1)
                half_column_units(i, 1, 5, 1)

                ahead = passes(b, AHEAD)
                c0 = 0
                for g, (size, (up_at, down_at)) in enumerate(zip(GROUPS, group_round)):
                    gate, up = gate_up_banks[g]
                    if g > 0:
                        pe.wait_ge(down_added.sem, down_added.after(b, (2 * g - 1) * NT))
                        pe.nop(nofuse=True)
                    with pe.Fori(1 if g == 0 else 0, size) as c:
                        chunk = b * NCH + c + c0
                        pe.wait_ge(silu_done.sem, silu_done.after(chunk))
                        column_units(first + c + up_at, 0, ps[:, gate, :])
                        pe.wait_ge(prod_done.sem, prod_done.after(chunk))
                        column_units(first + c + up_at, 1, ps[:, up, :])
                    if g > 0:
                        pe.wait_ge(down_added.sem, down_added.after(b, 2 * g * NT))
                    pe.wait_ge(hid_lo.sem, hid_lo.after(b * NCH, c0 + size - 1))
                    pe.nop(nofuse=True)
                    for n in range(2 * size):
                        half, k = divmod(n, size)
                        if n == size - 1:
                            pe.wait_ge(hid_lo.sem, hid_lo.after(b * NCH, c0 + size))
                        row_unit(first + down_at + n // 4, n % 4, act_hi, act_lo, k, down_bank(g, half), k == 0,
                                 k == size - 1, down_done)
                        if g == len(GROUPS) - 1 and half == 1 and k in TURN_AFTER:
                            if k == TURN_AFTER[0]:
                                pe.wait_ge(down_added.sem, down_added.after(b, (2 * g + 1) * NT))
                            turn_tile(ahead, TURN_AFTER.index(k), 4)
                        elif g == len(GROUPS) - 1 and half == 1 and k == LOW_RANK_AFTER:
                            low_rank(ahead)
                        elif g == len(GROUPS) - 1 and half == 1 and k == GATES_AFTER:
                            gates(ahead)
                    c0 += size

        @block.scalar
        def _(act):
            def split_hi(dst, src):
                return act.activation(dst, src, ACT.Copy)

            def root(n, cols=slice(0, NT)):
                act.wait_ge(variance_done.sem, variance_done.after(n, 1))
                act.activation(rstd[:, cols], variance[:, cols], ACT.Sqrt).then_inc(root_guess.sem, 1)

            def square(at, t, tile):
                if t > 0:
                    act.wait_ge(squared.sem, squared.after(at["squares"], t))
                act.activation(junk[:, :], tile, ACT.Square, accum_out=sumsq[:, t:t + 1]).then_inc(squared.sem, 1)

            def tile_root(at, t):
                root(at["roots"] + t, slice(t, t + 1))

            def turned_hi(at, t, bank0):
                act.wait_ge(xs_turned.sem, xs_turned.after(at["turn"], t + 1))
                for j in range(2):
                    split_hi(xT_hi[:, 4 * j:4 * j + 4, t * P:(t + 1) * P],
                             ps[:, bank0 + 2 * (t % 2) + j, :].rearrange("p (k n) -> p k n", n=P))\
                        .then_inc(xT_hi_done.sem, 1)

            def norm_turned(at, bank0, tile_there):
                for step, t in (("square", 0), ("root", 0), ("square", 1), ("root", 1), ("square", 2), ("split", 0),
                                ("split", 1), ("square", 3), ("root", 2), ("split", 2), ("split", 3)):
                    if step == "square":
                        tile_there(t)
                        square(at, t, h[:, t, :])
                    elif step == "root":
                        root(at["roots"] + t, slice(t, t + 1) if t < 2 else slice(2, NT))
                    else:
                        turned_hi(at, t, bank0)

            def load_x(rows, t):
                act.dma_start(xs[:, t % 2, :], x_tok[bass.ds(rows + t * P, P), :]).then_inc(x_in[t % 2].sem, 16)

            def square_x(at, t):
                act.wait_ge(x_in[t % 2].sem, x_in[t % 2].after(at["block"] - 1, t // 2 + 1))
                square(at, t, xs[:, t % 2, :])

            def look_ahead(at, rows):
                for t in range(2):
                    square_x(at, t)
                    tile_root(at, t)
                for t in range(2):
                    turned_hi(at, t, 4)
                    load_x(rows, t + 2)
                for t in (2, 3):
                    square_x(at, t)
                    tile_root(at, t)
                for t in (2, 3):
                    turned_hi(at, t, 4)

            def gates(at):
                n = at["block"]
                act.wait_ge(a_done.sem, a_done.after(n, 1))
                act.activation(aT[:, :], ps[0:6 * RANK, 6, :], ACT.Copy).then_inc(aT_hi_done.sem, 1)
                for hd in range(H):
                    act.wait_ge(z_done.sem, z_done.after(n, hd + 1))
                    act.activation(softlog[:, hd, :], ps[:, 4 + hd, :], ACT.Abs, bias=b_gate[:, hd:hd + 1])\
                        .then_inc(z_abs.sem, 1)
                act.wait_ge(z_abs.sem, z_abs.after(n, H))
                act.activation(softlog[:, :, :], softlog[:, :, :], ACT.Exp, scale=-1.0).then_inc(z_exp.sem, 1)
                act.wait_ge(z_exp.sem, z_exp.after(n, 1))
                act.activation(softlog[:, :, :], softlog[:, :, :], ACT.Ln, bias=1.0).then_inc(z_log.sem, 1)

            def decay_ends(at):
                n = at["block"]
                ends = lc[:, :, :].rearrange("p h (t c l) -> p h t c l", c=2, l=CHUNK)[:, :, :, :, CHUNK - 1]
                act.wait_ge(z_scan.sem, z_scan.after(n, H))
                act.wait_ge(odd_kept.sem, odd_kept.after(n, 1))
                act.activation(e_even[:, :, :], ends[:, :, :, 0], ACT.Exp, scale=1 / TAU).then_inc(ends_done.sem, 1)
                act.activation(e_odd[:, :, 1:], ends[:, :, :, 1], ACT.Exp, scale=1 / TAU).then_inc(ends_done.sem, 1)

            def make_decays(hh, hd):
                act.wait_ge(k_scaled.sem, k_scaled.after(hd))
                act.nop(nofuse=True)
                row = lc[:, bass.ds(hh, 1), :].rearrange("p a l -> p (a l)")
                act.activation(ef[:, :], row, ACT.Exp, scale=1 / TAU).then_inc(decays.sem, 1)
                act.activation(ei[:, :], row, ACT.Exp, scale=-1 / TAU).then_inc(decays.sem, 1)

            def head(b, hh, hd, i, last):
                act.wait_ge(kt_done.sem, kt_done.after(hd, 1))
                split_hi(k_hi[:, :], ps[:, 0, :]).then_inc(k_hi_done.sem, 1)
                act.wait_ge(past_done.sem, past_done.after(hd, 1))
                past = ps[:, 6, :].rearrange("p (t n) -> p t n", n=P)
                act.activation(scores[0:CHUNK, :, :], past[0:CHUNK, :, :], ACT.Copy).then_inc(past_copied.sem, 1)
                act.activation(scores[CHUNK:, :, CHUNK:], past[CHUNK:, :, CHUNK:], ACT.Copy)\
                    .then_inc(past_copied.sem, 1)
                act.wait_ge(scores_ready.sem, scores_ready.after(hd, 2))
                split_hi(scores_hi, scores[:, :, :]).then_inc(scores_hi_done.sem, 1)
                for j in range(2):
                    if j == 0:
                        act.wait_ge(vr_done.sem, vr_done.after(hd, 2))
                    else:
                        act.wait_ge(unit_used[3].sem, unit_used[3].after(i + 2, 1))
                    split_hi(v_hi[:, 2 * j:2 * j + 2, :], ps[:, 2 + 2 * j:4 + 2 * j, 0:DV]).then_inc(v_hi_done.sem, 1)
                act.wait_ge(v_done.sem, v_done.after(hd, 2))
                act.nop(nofuse=True)
                act.activation(r_gate[:, :, :], ps[:, 2:6, DV:], ACT.Silu).then_inc(r_silu.sem, 1)
                n = squares_pass(b, hh)
                for t in range(NT):
                    act.wait_ge(o_done.sem, o_done.after(hd, 2 * (t // 2) + 2))
                    if t > 0:
                        act.wait_ge(squared.sem, squared.after(n, t))
                    act.activation(junk[:, 0:DV], ps[:, 6 + t // 2, (t % 2) * DV:(t % 2 + 1) * DV], ACT.Square,
                                   accum_out=sumsq[:, t:t + 1]).then_inc(squared.sem, 1)
                root(root_number(b, hh))
                if not last:
                    make_decays(hh + 1, hd + 1)
                for j in range(2):
                    act.wait_ge(oT_done.sem, oT_done.after(hd, j + 1))
                    act.nop(nofuse=True)
                    split_hi(act_hi[:, bass.ds(2 * hh + j, 1), :].rearrange("p a l -> p (a l)"), ps[:, 6 + j, :])\
                        .then_inc(oT_hi.sem, 1)

            for sig in (*out_stored, silu_done, r_silu):
                sig.open(act)
            act.dma_start(g_mix[:, :], norm_mix_g.to_broadcast([P, D])).then_inc(mix_loaded.sem, 16)
            act.dma_start(wa_raw[:, :, :], a_w).then_inc(wa_loaded.sem, 16)
            with nc.allow_non_contiguous_dma(reason="512 numbers, once"):
                act.dma_start(b_gate[:, :], b_a[0].rearrange("(h p) -> p h", p=P)).then_inc(b_loaded.sem, 16)
            norm_turned(FIRST, 4, lambda t: act.wait_ge(first_loaded[t].sem, first_loaded[t].after(0, 1)))
            act.wait_ge(b_loaded.sem, b_loaded.after(0, 1))
            act.wait_ge(dve_init.sem, dve_init.after(0, 1))
            gates(FIRST)
            decay_ends(FIRST)
            act.wait_ge(lc_ready.sem, lc_ready.after(0, 1))
            make_decays(0, 0)

            with act.Fori(0, NB) as b:
                first = b * ROUNDS
                for t in range(NT):
                    act.dma_start(h[:, t, :], x_tok[bass.ds(b * T + t * P, P), :]).then_inc(h_loaded[t].sem, 16)
                act.wait_ge(out_stored[1].sem, out_stored[1].after(b))
                act.nop(nofuse=True)
                with act.Fori(0, H - 1) as hh:
                    head(b, hh, b * H + hh, first + hh * (PAIRS_HEAD // 2), False)
                head(b, H - 1, b * H + (H - 1), first + (H - 1) * (PAIRS_HEAD // 2), True)

                norm_turned(passes(b, FFN), 0, lambda t: act.wait_ge(wo_added.sem, wo_added.after(b, NT + t + 1)))
                load_x(next_rows(b), 0)
                load_x(next_rows(b), 1)

                c0 = 0
                for (gate, _), size, (up_at, _) in zip(gate_up_banks, GROUPS, group_round):
                    with act.Fori(0, size) as c:
                        chunk = b * NCH + c + c0
                        i = first + c + up_at
                        act.wait_ge(unit_used[1].sem, unit_used[1].after(i, 1))
                        act.wait_ge(prod_done.sem, prod_done.after(chunk))
                        act.activation(silu[:, :], ps[:, gate, :], ACT.Silu).then_inc(silu_done.sem, 1)
                        act.wait_ge(prod_done.sem, prod_done.after(chunk, 1))
                        act.nop(nofuse=True)
                        split_hi(act_hi[:, bass.ds(c, 1), :].rearrange("p a l -> p (a l)"), prod[:, :])\
                            .then_inc(hid_hi.sem, 1)
                    c0 += size

                look_ahead(passes(b, AHEAD), next_rows(b))
                gates(passes(b, AHEAD))
                at = passes(b, FINAL)
                for t in range(NT):
                    act.wait_ge(down_added.sem, down_added.after(b, 3 * NT + t + 1))
                    square(at, t, h[:, t, :])
                root(at["roots"])
                decay_ends(at)
                for t in range(NT):
                    act.wait_ge(xs_ready.sem, xs_ready.after(at["xs"], t + 1))
                    act.dma_start(out_tok[bass.ds(b * T + t * P, P), :], out_tiles[t])\
                        .then_inc(out_stored[t % 2].sem, 16)
                act.wait_ge(lc_ready.sem, lc_ready.after(b + 1, 1))
                make_decays(0, (b + 1) * H)
            for stored in out_stored:
                act.wait_ge(stored.sem, stored.after(NB))

        @block.vector
        def _(dve):
            def split_lo(dst, src, hi):
                return dve.tensor_tensor(dst, src, hi.bitcast(F32), ALU.subtract)

            def variance_of(n, size, passed, events, cols=slice(0, NT)):
                dve.wait_ge(squared.sem, squared.after(passed, events))
                dve.tensor_scalar(variance[:, cols], sumsq[:, cols], 1 / size, EPS, ALU.mult, ALU.add)\
                    .then_inc(variance_done.sem, 1)

            def root(n, cols=slice(0, NT)):
                dve.wait_ge(root_guess.sem, root_guess.after(n, 1))
                dve.reciprocal(rstd[:, cols], rstd[:, cols]).then_inc(newton_done.sem, 1)
                dve.wait_ge(newton_done.sem, newton_done.after(n, 1))
                dve.tensor_tensor(newton[:, cols], rstd[:, cols], rstd[:, cols], ALU.mult)\
                    .then_inc(newton_done.sem, 1)
                dve.wait_ge(newton_done.sem, newton_done.after(n, 2))
                dve.scalar_tensor_tensor(out=newton[:, cols], in0=newton[:, cols], scalar=-0.5, in1=variance[:, cols],
                                         op0=ALU.mult, op1=ALU.mult).then_inc(newton_done.sem, 1)
                dve.wait_ge(newton_done.sem, newton_done.after(n, 3))
                dve.scalar_tensor_tensor(out=rstd[:, cols], in0=newton[:, cols], scalar=1.5, in1=rstd[:, cols],
                                         op0=ALU.add, op1=ALU.mult).then_inc(rstd_ready.sem, 1)
                dve.wait_ge(rstd_ready.sem, rstd_ready.after(n, 1))

            def tile_variance(at, t):
                variance_of(at["roots"] + t, D, at["squares"], t + 1, slice(t, t + 1))

            def scale(at, t, tile, g):
                root(at["roots"] + t, slice(t, t + 1))
                scaled(xs[:, t % 2, :], tile, rstd[:, t:t + 1], g)

            def scaled(dst, tile, by, g):
                dve.scalar_tensor_tensor(out=dst, in0=tile, scalar=by, in1=g[:, :],
                                         op0=ALU.mult, op1=ALU.mult).then_inc(xs_ready.sem, 1)

            def turned_lo(at, t, bank0):
                for j in range(2):
                    dve.wait_ge(xT_hi_done.sem, xT_hi_done.after(at["turn"], 2 * t + j + 1))
                    blk = (slice(None), slice(4 * j, 4 * j + 4), slice(t * P, (t + 1) * P))
                    split_lo(xT_lo[blk], ps[:, bank0 + 2 * (t % 2) + j, :].rearrange("p (k n) -> p k n", n=P),
                             xT_hi[blk]).then_inc(xT_lo_done.sem, 1)

            def look_ahead_two(at):
                for t in range(2):
                    tile_variance(at, t)
                    scale(at, t, xs[:, t, :], g_mix)

            def look_ahead_rest(at):
                turned_lo(at, 0, 4)
                turned_lo(at, 1, 4)
                for t in (2, 3):
                    tile_variance(at, t)
                    scale(at, t, xs[:, t % 2, :], g_mix)
                for t in (2, 3):
                    turned_lo(at, t, 4)

            def norm_turned(at, bank0, g, steps, add=None, xs_free=None):
                for step, t in steps:
                    if step == "add":
                        add(t)
                    elif step == "variance":
                        tiles = slice(t, t + 1) if t < 2 else slice(2, NT)
                        variance_of(at["roots"] + t, D, at["squares"], tiles.stop, tiles)
                    elif step == "root":
                        root(at["roots"] + t, slice(t, t + 1) if t < 2 else slice(2, NT))
                    elif step == "scale":
                        if t >= 2:
                            dve.wait_ge(xs_turned.sem, xs_turned.after(at["turn"], t - 1))
                        elif xs_free is not None:
                            xs_free(t)
                        scaled(xs[:, t % 2, :], h[:, t, :], rstd[:, t:t + 1], g)
                    else:
                        turned_lo(at, t, bank0)

            chunks = lc[:, :, :].rearrange("p h (t c l) -> p (h t) c l", c=2, l=CHUNK)

            def gates_min(at):
                dve.wait_ge(aT_hi_done.sem, aT_hi_done.after(at["block"], 1))
                last = slice(4 * RANK, 6 * RANK)
                split_lo(aT[last, :], ps[last, 6, :], aT[last, :]).then_inc(aT_done.sem, 1)
                for hd in range(H):
                    dve.wait_ge(z_abs.sem, z_abs.after(at["block"], hd + 1))
                    dve.tensor_scalar(lc[:, hd, :], ps[:, 4 + hd, :], b_gate[:, hd:hd + 1], 0.0, ALU.add, ALU.min)\
                        .then_inc(z_min.sem, 1)

            def gates_sum(at):
                n = at["block"]
                dve.wait_ge(z_min.sem, z_min.after(n, H))
                dve.wait_ge(z_log.sem, z_log.after(n, 1))
                dve.tensor_tensor(lc[:, :, :], lc[:, :, :], softlog[:, :, :], ALU.subtract).then_inc(z_sub.sem, 1)
                dve.wait_ge(z_sub.sem, z_sub.after(n, 1))
                for hd in range(H):
                    dve.tensor_tensor_scan(lc[:, hd, :], carry_mask[:, :], lc[:, hd, :], 0.0, ALU.mult,
                                           ALU.add).then_inc(z_scan.sem, 1)

            def keep_ends(at):
                n = at["block"]
                dve.wait_ge(z_scan.sem, z_scan.after(n, H))
                dve.tensor_copy(e_odd[:, :, 0:1], e_odd[:, :, NT:]).then_inc(odd_kept.sem, 1)
                dve.tensor_copy(lend[:, :], chunks[:, :, 0, CHUNK - 1]).then_inc(lend_done.sem, 1)

            def from_border(at):
                n = at["block"]
                dve.wait_ge(lend_done.sem, lend_done.after(n, 1))
                dve.wait_ge(ends_done.sem, ends_done.after(n, 2))
                dve.tensor_tensor(chunks[:, :, 0, :], chunks[:, :, 0, :],
                                  lend[:, :].unsqueeze(2).to_broadcast([P, H * NT, CHUNK]),
                                  ALU.subtract).then_inc(lc_ready.sem, 1)

            def add_tile(b, done, n, last_unit, last_round, half, bank0, t, added):
                if t < NT - 1:
                    dve.wait_ge(done.sem, done.after(b, n + t + 1))
                else:
                    dve.wait_ge(unit_used[last_unit].sem, unit_used[last_unit].after(last_round, 1))
                part = h[:, t, half * HALF:(half + 1) * HALF]
                dve.tensor_tensor(part, part, ps[:, bank0 + t, :], ALU.add).then_inc(added.sem, 1)

            def scale_qk(hd, i):
                dve.wait_ge(decays.sem, decays.after(hd, 2))
                dve.wait_ge(o_done.sem, o_done.after(hd))
                dve.wait_ge(unit_used[1].sem, unit_used[1].after(i, 1))
                dve.scalar_tensor_tensor(out=qf, in0=ps[:, 0, :], scalar=DK ** -0.5, in1=ef[:, :], op0=ALU.mult,
                                         op1=ALU.mult).then_inc(q_scaled.sem, 1)
                dve.scalar_tensor_tensor(out=qb, in0=ps[:, 0, :], scalar=DK ** -0.5, in1=ei[:, :], op0=ALU.mult,
                                         op1=ALU.mult).then_inc(q_scaled.sem, 1)
                dve.wait_ge(unit_used[3].sem, unit_used[3].after(i, 1))
                dve.tensor_tensor(kf, ps[:, 1, :], ei[:, :], ALU.mult).then_inc(k_scaled.sem, 1)
                dve.tensor_tensor(kb, ps[:, 1, :], ef[:, :], ALU.mult).then_inc(k_scaled.sem, 1)

            def gate_r(hh, hd):
                dve.wait_ge(r_silu.sem, r_silu.after(hd, 1))
                dve.tensor_tensor(r_gate[:, :, :], r_gate[:, :, :],
                                  g_gla[:, bass.ds(hh * DV, DV)].unsqueeze(1).to_broadcast([P, NT, DV]),
                                  ALU.mult).then_inc(r_done.sem, 1)

            def head(b, hh, hd, i, last):
                dve.wait_ge(k_hi_done.sem, k_hi_done.after(hd, 1))
                dve.nop(nofuse=True)
                split_lo(k_lo, ps[:, 0, :], k_hi[:, :]).then_inc(k_tok_done.sem, 1)
                dve.wait_ge(future_done.sem, future_done.after(hd, 1))
                dve.wait_ge(past_copied.sem, past_copied.after(hd, 2))
                dve.nop(nofuse=True)
                back = ps[:, 7, :].rearrange("p (t n) -> p t n", n=P)
                for c in range(2):
                    part = (slice(c * CHUNK, (c + 1) * CHUNK), slice(None), slice(c * CHUNK, (c + 1) * CHUNK))
                    dve.copy_predicated(scores[part], future[c * CHUNK:(c + 1) * CHUNK, :, :], back[part])\
                        .then_inc(scores_ready.sem, 1)
                dve.wait_ge(scores_hi_done.sem, scores_hi_done.after(hd, 1))
                split_lo(scores_lo, scores[:, :, :], scores_hi).then_inc(scores_split.sem, 1)

                mine = state[:, bass.ds(hh, 1), :].rearrange("p a v -> p (a v)")
                for t in range(NT):
                    if t > 0:
                        dve.wait_ge(state_done.sem, state_done.after(hd, t))
                    dve.tensor_scalar(state_in[:, t, :], mine,
                                      e_odd[:, bass.ds(hh, 1), t:t + 1].rearrange("p a t -> p (a t)"),
                                      e_even[:, bass.ds(hh, 1), t:t + 1].rearrange("p a t -> p (a t)"), ALU.mult,
                                      ALU.mult).then_inc(state_in_done.sem, 1)
                    if t == 0:
                        for j in range(2):
                            dve.wait_ge(v_hi_done.sem, v_hi_done.after(hd, j + 1))
                            two = slice(2 * j, 2 * j + 2)
                            split_lo(v_lo[:, two, :], ps[:, 2 + 2 * j:4 + 2 * j, 0:DV], v_hi[:, two, :])\
                                .then_inc(v_done.sem, 1)
                        if not last:
                            gate_r(hh, hd)
                    dve.wait_ge(state_in_done.sem, state_in_done.after(hd, t + 1))
                    dve.wait_ge(ds_done.sem, ds_done.after(hd, 2 * (t // 2) + 2))
                    dve.tensor_tensor(mine, state_in[:, t, :], ps[:, 1, (t % 2) * DV:(t % 2 + 1) * DV],
                                      ALU.add).then_inc(state_done.sem, 1)
                if last:
                    gate_r(hh, hd)
                variance_of(root_number(b, hh), DV, squares_pass(b, hh), NT)
                root(root_number(b, hh))
                dve.wait_ge(r_done.sem, r_done.after(hd, 1))
                for t in range(NT):
                    dve.scalar_tensor_tensor(out=og[:, t, :], in0=ps[:, 6 + t // 2, (t % 2) * DV:(t % 2 + 1) * DV],
                                             scalar=rstd[:, t:t + 1], in1=r_gate[:, t, :], op0=ALU.mult,
                                             op1=ALU.mult).then_inc(og_done.sem, 1)
                if not last:
                    scale_qk(hd + 1, i + 3)
                for j in range(2):
                    dve.wait_ge(oT_hi.sem, oT_hi.after(hd, j + 1))
                    split_lo(act_lo[:, bass.ds(2 * hh + j, 1), :].rearrange("p a l -> p (a l)"), ps[:, 6 + j, :],
                             act_hi[:, bass.ds(2 * hh + j, 1), :].rearrange("p a l -> p (a l)"))\
                        .then_inc(oT_lo.sem, 1)

            for sig in (oT_lo, prod_done, k_scaled, hid_lo, down_added):
                sig.open(dve)
            dve.memset(scores[:, :, :], 0.0)
            dve.memset(state[:, :, :], 0.0)
            dve.memset(e_odd[:, :, :], 1.0).then_inc(dve_init.sem, 1)
            dve.wait_ge(dve_init.sem, dve_init.after(0, 1))
            dve.wait_ge(mix_loaded.sem, mix_loaded.after(0, 1))
            norm_turned(FIRST, 4, g_mix, (("variance", 0), ("root", 0), ("scale", 0), ("variance", 1), ("root", 1),
                                          ("scale", 1), ("split", 0), ("split", 1), ("variance", 2), ("root", 2),
                                          ("scale", 2), ("scale", 3), ("split", 2), ("split", 3)))
            dve.wait_ge(b_loaded.sem, b_loaded.after(0, 1))
            dve.wait_ge(norms_loaded.sem, norms_loaded.after(0, 3))
            dve.wait_ge(masks.sem, masks.after(0, 1))
            gates_min(FIRST)
            gates_sum(FIRST)
            keep_ends(FIRST)
            from_border(FIRST)

            with dve.Fori(0, NB) as b:
                first = b * ROUNDS
                scale_qk(b * H, first)
                dve.wait_ge(out_stored[0].sem, out_stored[0].after(b))
                dve.nop(nofuse=True)
                with dve.Fori(0, H - 1) as hh:
                    head(b, hh, b * H + hh, first + hh * (PAIRS_HEAD // 2), False)
                head(b, H - 1, b * H + (H - 1), first + (H - 1) * (PAIRS_HEAD // 2), True)

                for t in range(NT):
                    dve.wait_ge(h_loaded[t].sem, h_loaded[t].after(b, 1))
                    add_tile(b, wo_done, 0, 3, first + ROUND_OUT + 1, 0, 0, t, wo_added)
                norm_turned(passes(b, FFN), 0, g_ffn,
                            (("add", 0), ("variance", 0), ("root", 0), ("add", 1), ("scale", 0), ("variance", 1),
                             ("add", 2), ("root", 1), ("scale", 1), ("split", 0), ("add", 3), ("split", 1),
                             ("variance", 2), ("root", 2), ("scale", 2), ("scale", 3), ("split", 2), ("split", 3)),
                            lambda t: add_tile(b, wo_done, NT - 1, 3, first + ROUND_OUT + 3, 1, 4, t, wo_added),
                            lambda t: dve.wait_ge(out_stored[t].sem, out_stored[t].after(b)))

                ahead = passes(b, AHEAD)
                c0 = 0
                for g, (size, (up_at, down_at)) in enumerate(zip(GROUPS, group_round)):
                    with dve.Fori(0, size) as c:
                        chunk = b * NCH + c + c0
                        dve.wait_ge(silu_done.sem, silu_done.after(chunk, 1))
                        dve.wait_ge(unit_used[3].sem, unit_used[3].after(first + c + up_at, 1))
                        dve.wait_ge(hid_lo.sem, hid_lo.after(chunk))
                        dve.tensor_tensor(prod[:, :], silu[:, :], ps[:, gate_up_banks[g][1], :],
                                          ALU.mult).then_inc(prod_done.sem, 1)
                        dve.wait_ge(hid_hi.sem, hid_hi.after(chunk, 1))
                        split_lo(act_lo[:, bass.ds(c, 1), :].rearrange("p a l -> p (a l)"), prod[:, :],
                                 act_hi[:, bass.ds(c, 1), :].rearrange("p a l -> p (a l)")).then_inc(hid_lo.sem, 1)
                    if g == len(GROUPS) - 1:
                        look_ahead_two(ahead)
                    for half in range(2):
                        n = (half + 1) * size - 1
                        for t in range(NT):
                            add_tile(b, down_done, (2 * g + half) * (NT - 1), n % 4, first + down_at + n // 4, half,
                                     down_bank(g, half), t, down_added)
                        if g == len(GROUPS) - 1 and half == 0:
                            look_ahead_rest(ahead)
                            gates_min(ahead)
                    c0 += size
                gates_sum(ahead)

                at = passes(b, FINAL)
                variance_of(at["roots"], D, at["squares"], NT)
                keep_ends(ahead)
                root(at["roots"])
                dve.wait_ge(xs_turned.sem, xs_turned.after(ahead["turn"], NT))
                for t in range(NT):
                    scaled(out_tiles[t], h[:, t, :], rstd[:, t:t + 1], g_fin)
                from_border(ahead)


_INS = ["x", "norm_mix_g", "norm_ffn_g", "gla_w_in", "gla_w_a2", "gla_b_a", "gla_norm_g", "gla_w_out", "ffn_w_gu",
        "ffn_w_down", "final_norm_g"]


def kernel(**inputs):
    import numpy as np
    import concourse.bacc as bacc
    from concourse.bass_utils import run_bass_kernel_spmd

    nc = bacc.Bacc("TRN2", target_bir_lowering=False, num_devices=1)
    arrays, args = {}, []
    for name in _INS:
        a = np.ascontiguousarray(inputs[name])
        arrays[f"in_{name}"] = a
        args.append(nc.dram_tensor(f"in_{name}", a.shape, mybir.dt.from_np(a.dtype), kind="ExternalInput").ap())
    args.append(nc.dram_tensor("out_0", inputs["x"].shape, F32, kind="ExternalOutput").ap())
    gla_layer(nc, *args)
    return run_bass_kernel_spmd(nc, [arrays], core_ids=[0]).results[0]["out_0"]
```
